# Optimizing a Trainium2 kernel written in Bass

```python
import jax, jax.numpy as jnp
from jax import lax
import numpy as np

D_MODEL = 1024
BATCH = 1
SEQ = 512
DEPTH = 1

HEAD_DIM = 64
A_HEADS = 8
A_WIDTH = A_HEADS * HEAD_DIM
DECAY_LORA = 64
ICLR_LORA = 64
GATE_LORA = 160
GN_EPS = 64e-5
B_HEADS = 8
B_WIDTH = B_HEADS * HEAD_DIM
MOBA_BLOCK = 256
MOBA_TOP_K = 3
MOBA_Q_CHUNK = 16
FFN_HIDDEN = ((8 * D_MODEL // 3 + 255) // 256) * 256
RMS_EPS = 1e-6
SHIFT_WIDTH = 3 * A_WIDTH + DECAY_LORA + ICLR_LORA + GATE_LORA
PROJ_WIDTH = SHIFT_WIDTH + 3 * B_WIDTH + 2 * D_MODEL

kernel_name = "hybrid_rwkv7_moba_gated_block"

def _split(t, sizes):
    return jnp.split(t, [int(s) for s in np.cumsum(sizes)[:-1]], axis=-1)

def rms_norm(x, g):
    xf = x.astype(jnp.float32)
    y = xf * lax.rsqrt(jnp.mean(xf * xf, axis=-1, keepdims=True) + RMS_EPS)
    return (y * g.astype(jnp.float32)).astype(x.dtype)

def token_shift_mix(p, mu):
    prev = jnp.pad(p, ((0, 0), (1, 0), (0, 0)))[:, :-1]
    return p + mu * (prev - p)

def alibi_slopes(n_heads):
    return jnp.exp2(-8.0 * jnp.arange(1, n_heads + 1, dtype=jnp.float32) / n_heads)

def rwkv7_time_mix(r, k, v, wd, ad, gd, w0, w_decay_up, a0, w_iclr_up, w_gate_up,
                   k_k, k_a, r_k, ln_w, ln_b):
    B_, S_, _ = r.shape
    w_log = -jax.nn.softplus(-(w0 + jnp.tanh(wd) @ w_decay_up)) - 0.5
    decay = jnp.exp(-jnp.exp(w_log.astype(jnp.float32))).astype(r.dtype)
    a = jax.nn.sigmoid(a0 + ad @ w_iclr_up)
    g = jax.nn.sigmoid(gd) @ w_gate_up

    def heads(t):
        return t.reshape(B_, S_, A_HEADS, HEAD_DIM)

    kkf = heads(k * k_k).astype(jnp.float32)
    kk = (kkf / jnp.maximum(jnp.linalg.norm(kkf, axis=-1, keepdims=True), 1e-12)).astype(k.dtype)
    k = k * (1.0 + (a - 1.0) * k_a)
    rh, wh, kh, vh, ah = heads(r), heads(decay), heads(k), heads(v), heads(a)

    def step(state, inp):
        r_t, w_t, k_t, v_t, kk_t, a_t = inp
        sa = jnp.einsum('bhij,bhj->bhi', state, -kk_t)
        state = (state * w_t[:, :, None, :]
                 + sa[..., None] * (kk_t * a_t)[:, :, None, :]
                 + v_t[..., None] * k_t[:, :, None, :])
        y_t = jnp.einsum('bhij,bhj->bhi', state, r_t)
        return state, y_t

    xs = tuple(jnp.moveaxis(t, 1, 0) for t in (rh, wh, kh, vh, kk, ah))
    s0 = jnp.zeros((B_, A_HEADS, HEAD_DIM, HEAD_DIM), r.dtype)
    _, y = lax.scan(step, s0, xs)
    y = jnp.moveaxis(y, 0, 1)
    yf = y.astype(jnp.float32)
    mean = jnp.mean(yf, axis=-1, keepdims=True)
    var = jnp.mean(jnp.square(yf - mean), axis=-1, keepdims=True)
    y = ((yf - mean) * lax.rsqrt(var + GN_EPS)).astype(r.dtype).reshape(B_, S_, A_WIDTH)
    y = y * ln_w + ln_b
    bonus = jnp.sum(rh * kh * r_k, axis=-1, keepdims=True) * vh
    return (y + bonus.reshape(B_, S_, A_WIDTH)) * g

def moba_attention(q, k, v):
    B_, S_, _ = q.shape
    scale = HEAD_DIM ** -0.5

    def heads(t):
        return t.reshape(B_, S_, B_HEADS, HEAD_DIM).transpose(0, 2, 1, 3)

    q, k, v = heads(q), heads(k), heads(v)
    nb = -(-S_ // MOBA_BLOCK)
    pad = ((0, 0), (0, 0), (0, nb * MOBA_BLOCK - S_), (0, 0))
    kb = jnp.pad(k, pad).reshape(B_, B_HEADS, nb, MOBA_BLOCK, HEAD_DIM)
    vb = jnp.pad(v, pad).reshape(B_, B_HEADS, nb, MOBA_BLOCK, HEAD_DIM)

    k_mean = jnp.mean(kb.astype(jnp.float32), axis=3)
    gate = jnp.einsum('bhsd,bhnd->bhsn', q.astype(jnp.float32), k_mean)
    q_block = jnp.arange(S_) // MOBA_BLOCK
    fully_past = jnp.arange(nb)[None, :] < q_block[:, None]
    gate = jnp.where(fully_past, gate, -jnp.inf)
    n_sel = min(MOBA_TOP_K, nb)
    _, idx = lax.top_k(gate, n_sel)
    slopes = alibi_slopes(B_HEADS)
    gather_blocks = jax.vmap(jax.vmap(lambda blocks, ids: blocks[ids]))

    def chunk_fn(args):
        q_c, idx_c, t0 = args
        t = t0 + jnp.arange(MOBA_Q_CHUNK, dtype=jnp.int32)
        blk = t0 // MOBA_BLOCK
        k_sel = gather_blocks(kb, idx_c)
        v_sel = gather_blocks(vb, idx_c)
        s_sel = jnp.einsum('bhcd,bhcjkd->bhcjk', q_c, k_sel).astype(jnp.float32) * scale
        pos_sel = idx_c[..., None] * MOBA_BLOCK + jnp.arange(MOBA_BLOCK, dtype=jnp.int32)
        dist_sel = (t[:, None, None] - pos_sel).astype(jnp.float32)
        valid = jnp.arange(n_sel) < jnp.minimum(blk, n_sel)
        s_sel = jnp.where(valid[:, None], s_sel - slopes.reshape(1, -1, 1, 1, 1) * dist_sel, -jnp.inf)
        k_own = lax.dynamic_index_in_dim(kb, blk, axis=2, keepdims=False)
        v_own = lax.dynamic_index_in_dim(vb, blk, axis=2, keepdims=False)
        s_own = jnp.einsum('bhcd,bhkd->bhck', q_c, k_own).astype(jnp.float32) * scale
        dist_own = t[:, None] - (blk * MOBA_BLOCK + jnp.arange(MOBA_BLOCK, dtype=jnp.int32))[None, :]
        s_own = jnp.where(dist_own >= 0,
                          s_own - slopes.reshape(1, -1, 1, 1) * dist_own.astype(jnp.float32),
                          -jnp.inf)
        n_past = n_sel * MOBA_BLOCK
        scores = jnp.concatenate([s_sel.reshape(*s_sel.shape[:3], n_past), s_own], axis=-1)
        p = jax.nn.softmax(scores, axis=-1).astype(v_sel.dtype)
        p_sel = p[..., :n_past].reshape(s_sel.shape)
        p_own = p[..., n_past:]
        return (jnp.einsum('bhcjk,bhcjkd->bhcd', p_sel, v_sel)
                + jnp.einsum('bhck,bhkd->bhcd', p_own, v_own))

    n_chunks = S_ // MOBA_Q_CHUNK

    def to_chunks(t):
        return jnp.moveaxis(t.reshape(B_, B_HEADS, n_chunks, MOBA_Q_CHUNK, *t.shape[3:]), 2, 0)

    t0s = jnp.arange(n_chunks, dtype=jnp.int32) * MOBA_Q_CHUNK
    out = lax.map(chunk_fn, (to_chunks(q), to_chunks(idx), t0s))
    out = jnp.moveaxis(out, 0, 2).reshape(B_, B_HEADS, S_, HEAD_DIM)
    return out.transpose(0, 2, 1, 3).reshape(B_, S_, B_WIDTH)

def setup_inputs(seed: int = 0) -> dict:
    key = jax.random.key(seed)
    ks = jax.random.split(key, 22)
    L = DEPTH
    f32 = jnp.float32

    def nrm(k, shape, scale):
        return jax.random.normal(k, shape, f32) * scale

    return {
        "x": nrm(ks[0], (BATCH, SEQ, D_MODEL), 1.0),
        "norm_mix_g": 1.0 + nrm(ks[1], (L, D_MODEL), 0.02),
        "w_in": nrm(ks[2], (L, D_MODEL, PROJ_WIDTH), D_MODEL ** -0.5),
        "mu_shift": jax.random.uniform(ks[3], (L, SHIFT_WIDTH), f32),
        "w0": jax.random.uniform(ks[4], (L, A_WIDTH), f32, -6.0, 0.0),
        "w_decay_up": nrm(ks[5], (L, DECAY_LORA, A_WIDTH), 0.5 * DECAY_LORA ** -0.5),
        "a0": nrm(ks[6], (L, A_WIDTH), 0.5),
        "w_iclr_up": nrm(ks[7], (L, ICLR_LORA, A_WIDTH), ICLR_LORA ** -0.5),
        "w_gate_up": nrm(ks[8], (L, GATE_LORA, A_WIDTH), GATE_LORA ** -0.5),
        "k_k": 0.85 + nrm(ks[9], (L, A_WIDTH), 0.05),
        "k_a": 1.0 + nrm(ks[10], (L, A_WIDTH), 0.05),
        "r_k": nrm(ks[11], (L, A_HEADS, HEAD_DIM), 0.1),
        "ln_x_w": 1.0 + nrm(ks[12], (L, A_WIDTH), 0.02),
        "ln_x_b": nrm(ks[13], (L, A_WIDTH), 0.02),
        "w_up_a": nrm(ks[14], (L, A_WIDTH, D_MODEL), A_WIDTH ** -0.5),
        "w_up_b": nrm(ks[15], (L, B_WIDTH, D_MODEL), B_WIDTH ** -0.5),
        "w_o": nrm(ks[16], (L, D_MODEL, D_MODEL), D_MODEL ** -0.5),
        "norm_ffn_g": 1.0 + nrm(ks[17], (L, D_MODEL), 0.02),
        "w_ffn_in": nrm(ks[18], (L, D_MODEL, 2 * FFN_HIDDEN), D_MODEL ** -0.5),
        "w_ffn_out": nrm(ks[19], (L, FFN_HIDDEN, D_MODEL), FFN_HIDDEN ** -0.5),
        "norm_final_g": 1.0 + nrm(ks[20], (D_MODEL,), 0.02),
    }

def reference(x, norm_mix_g, w_in, mu_shift, w0, w_decay_up, a0, w_iclr_up, w_gate_up,
              k_k, k_a, r_k, ln_x_w, ln_x_b, w_up_a, w_up_b, w_o, norm_ffn_g,
              w_ffn_in, w_ffn_out, norm_final_g):
    for l in range(DEPTH):
        h = rms_norm(x, norm_mix_g[l])
        proj = h @ w_in[l]
        shift_part, q_b, k_b, v_b, gate_a, gate_b = _split(
            proj, [SHIFT_WIDTH, B_WIDTH, B_WIDTH, B_WIDTH, D_MODEL, D_MODEL])
        shift_part = token_shift_mix(shift_part, mu_shift[l])
        r_a, k_a_in, v_a, wd, ad, gd = _split(
            shift_part, [A_WIDTH, A_WIDTH, A_WIDTH, DECAY_LORA, ICLR_LORA, GATE_LORA])
        y_a = rwkv7_time_mix(r_a, k_a_in, v_a, wd, ad, gd, w0[l], w_decay_up[l], a0[l],
                             w_iclr_up[l], w_gate_up[l], k_k[l], k_a[l], r_k[l],
                             ln_x_w[l], ln_x_b[l]) @ w_up_a[l]
        y_b = moba_attention(q_b, k_b, v_b) @ w_up_b[l]
        mixed = jax.nn.sigmoid(gate_a) * y_a + jax.nn.sigmoid(gate_b) * y_b
        x = x + mixed @ w_o[l]
        h = rms_norm(x, norm_ffn_g[l])
        g_ff, u_ff = _split(h @ w_ffn_in[l], [FFN_HIDDEN, FFN_HIDDEN])
        x = x + (jax.nn.silu(g_ff) * u_ff) @ w_ffn_out[l]
    return rms_norm(x, norm_final_g)


_drawn_inputs = setup_inputs


def setup_inputs(seed=0):
    import zlib

    import numpy as np

    out = dict(_drawn_inputs(seed))
    spreads = {}
    factors = {'norm_mix_g': 3.801,
     'w_decay_up': 7.212,
     'k_k': 27.079,
     'k_a': 3.041,
     'ln_x_w': 61.998,
     'ln_x_b': 59.278,
     'norm_ffn_g': 11.659,
     'norm_final_g': 8.763}
    for name, (base, spread) in spreads.items():
        noise = np.random.default_rng([zlib.crc32(name.encode()), seed]).standard_normal(out[name].shape)
        drawn = base * np.exp(spread * noise) if base else spread * noise
        out[name] = __import__('jax').numpy.asarray(drawn.astype(out[name].dtype))
    for name, factor in factors.items():
        out[name] = (out[name] * factor).astype(out[name].dtype)
    return out
```

```python
from contextlib import ExitStack

import concourse.bass as bass
from concourse import mybir

F32 = mybir.dt.float32
F32R = mybir.dt.float32r
U32 = mybir.dt.uint32
ALU = mybir.AluOpType
ACT = mybir.ActivationFunctionType
AX = mybir.AxisListType

P = 128
D = 1024
T = 512
KD = D // P
TT = T // P
HD = 64
AW = 512
NP_ = AW // P
NH = AW // HD
GL = 160
GH = GL // 2
F = 2816
FT = F // P
RMS_EPS = 1e-6
GN_EPS = 64e-5
CDEC = 0.6065306597126334
BIG = 1e30
LEVELS = [2, 4, 8, 16, 32, 64]

C_R, C_K, C_V = 0, 512, 1024
C_WD, C_GD = 1536, 1664
C_Q = 1824
C_KB, C_VB = C_Q + 512, C_Q + 1024
C_GA = C_Q + 1536
C_GB = C_GA + D

U_LORA = 0
U_RKV = 3
U_QK = 15
U_VB = 23
U_GU = 27
U_WO = 51
U_FI = 59
U_FO = 103
N_UNITS = U_FO + FT
N_SHIFT = 15
RKV_TILE = [4, 5, 6, 7, 0, 1, 2, 3, 8, 9, 10, 11]
VB_BANK = [0, 5, 6, 7]
NRAW = 4
NSPL = 2

PC = {}
_at = 0
for _n, _k in (("mu", 12), ("mu_wa", 1), ("mu_g", 2), ("w0", 4), ("a0", 4), ("k_k", 4), ("k_a", 4),
               ("r_k", 4), ("ln_w", 4), ("ln_b", 4), ("g_mix", 8), ("g_ffn", 8)):
    PC[_n] = (_at, _k)
    _at += _k
NPAR = _at


def build(nc, x, norm_mix_g, w_in, mu_shift, w0, w_decay_up, a0, w_iclr_up, w_gate_up, k_k, k_a, r_k,
          ln_x_w, ln_x_b, w_up_a, w_up_b, w_o, norm_ffn_g, w_ffn_in, w_ffn_out, norm_final_g, out):
    xd = x[0].rearrange("(t p) d -> p t d", p=P)
    outd = out[0].rearrange("(t p) d -> p t d", p=P)
    w_in, w_up_a, w_up_b, w_o = w_in[0], w_up_a[0], w_up_b[0], w_o[0]
    w_ffn_in, w_ffn_out = w_ffn_in[0], w_ffn_out[0]

    with ExitStack() as ctx:
        at = [(nc.sbuf_base + 31) // 32 * 32]
        top = [0]

        def sb(name, shape, dt=F32):
            t = nc.alloc_sbuf_tensor_at(name, shape, dt, offset=at[0])
            n = 4
            for s in shape[1:]:
                n *= s
            at[0] += (n + 31) // 32 * 32
            top[0] = max(top[0], at[0])
            assert at[0] <= nc.sbuf_usable_end, (name, at[0])
            return t

        def sem(name):
            return ctx.enter_context(nc.semaphore(name))

        PS = ctx.enter_context(nc.psum_tensor("PS", [P, 8, 512], F32))

        ident = sb("ident", [P, P])
        blk1 = sb("blk1", [P, P])
        par = sb("par", [P, NPAR])
        qk_dram = nc.dram_tensor("qk_scratch", (2 * NP_, P, T), F32).ap()
        omka = sb("omka", [P, 4])
        hT_hi = sb("hT_hi", [P, KD, T], F32R)
        hT_lo = sb("hT_lo", [P, KD, T], F32R)
        wraw = sb("wraw", [P, NRAW, 1024])
        w_hi = sb("w_hi", [P, NSPL, 1024], F32R)
        w_lo = sb("w_lo", [P, NSPL, 1024], F32R)
        ss = sb("ss", [P, 3, TT])
        rstd = sb("rstd", [P, 3, TT])
        base = at[0]

        yaT_hi = sb("yaT_hi", [P, NP_, T], F32R)
        yaT_lo = sb("yaT_lo", [P, NP_, T], F32R)
        mixers = at[0]
        at[0] = base
        raw = sb("raw", [P, 2, 516])
        rawd = sb("rawd", [P, 2, 512])
        lmix = sb("lmix", [P, 3, 512])
        assert at[0] <= mixers
        at[0] = base
        stage = sb("stage", [P, 2, NP_, T])
        at[0] = mixers

        xt = sb("xt", [P, TT, D])
        xn = sb("xn", [P, TT, D])
        junk = sb("junk", [P, D])
        prow = sb("prow", [P, P])
        tmpi = sb("tmpi", [P, P])

        at[0] = mixers
        rkvT = sb("rkvT", [P, 12, T])
        wupda = sb("wupda", [P, AW])
        wupg = sb("wupg", [GH, 2, AW])
        loraT = sb("loraT", [P, T])
        gdT = sb("gdT", [GH, 2, T])
        m_st = sb("m_st", [P, P])
        m_si = sb("m_si", [P, 2, P])
        lmask = sb("lmask", [P, 6, P])
        umask = sb("umask", [P, HD])
        resets = sb("resets", [P, 4 * P])
        kkE_R = sb("kkE_R", [P, 2, NP_, 2, P])
        Bt = sb("Bt", [P, NP_, P])
        Kt = sb("Kt", [P, NP_, P])
        V_tok = sb("V_tok", [P, AW])
        B_tok = sb("B_tok", [P, AW])
        K_tok = sb("K_tok", [P, AW])
        M_ts = sb("M_ts", [P, NH, P])
        MT_rb = sb("MT_rb", [P, NH, 2, P])
        LK_rk = sb("LK_rk", [P, NH, 2, P])
        Tm = sb("Tm", [P, NH, P])
        TmT = sb("TmT", [P, NH, P])
        PR = sb("PR", [P, 2, 4, P])
        G_sb = PR[:, 0].rearrange("p h (two d) -> p (h two) d", two=2)
        U_sb = sb("U_sb", [P, NH, HD])
        S_sb = sb("S_sb", [P, NP_, HD])
        S_tmp = sb("S_tmp", [P, NP_, HD])
        sg = sb("sg", [P, NP_, P])
        X = sb("X", [P, NP_, P])
        x63 = sb("x63", [P, NP_])
        gmid = sb("gmid", [P, NP_])
        gend = sb("gend", [P, NP_])
        gg = sb("gg", [P, NP_])
        Ep = sb("Ep", [P, NP_, P])
        Ee = sb("Ee", [P, NP_, P])
        En = sb("En", [P, NP_, P])
        aT = sb("aT", [P, NP_, P])
        kk = sb("kk", [P, NP_, P])
        sq = sb("sq", [P, NP_, P])
        rinv = sq
        kp = sb("kp", [P, NP_, P])
        rk = sb("rk", [P, NP_, P])
        bonv = sb("bonv", [P, NP_, P])
        gsb = sb("gsb", [P, NP_, P])
        ysum = sb("ysum", [P, NH])
        yvar = sb("yvar", [P, NH])
        yc = sb("yc", [P, NH, HD])
        yT = sb("yT", [P, NP_, P])
        ysq = yT[:].rearrange("p a (b d) -> p (a b) d", d=HD)

        at[0] = mixers
        obT_hi = sb("obT_hi", [P, NP_, T], F32R)
        obT_lo = sb("obT_lo", [P, NP_, T], F32R)
        mixed = at[0]
        V_b = sb("V_b", [P, TT, AW])
        qkT = sb("qkT", [P, 2 * NP_, T])
        dist = sb("dist", [P, T])
        alibi = sb("alibi", [P, 2, T])
        sc = sb("sc", [P, 2, T])
        Pr = sb("Pr", [P, 2, T])
        PT = sb("PT", [P, 2, TT, P])
        nmax = sb("nmax", [P, 2, TT])
        rsum = sb("rsum", [P, 2, TT])
        rrec = sb("rrec", [P, 2, TT])
        O_sb = sb("O_sb", [P, TT, P])
        obf = sb("obf", [P, T])

        at[0] = mixed
        mixT_hi = sb("mixT_hi", [P, KD, T], F32R)
        mixT_lo = sb("mixT_lo", [P, KD, T], F32R)
        sgate = sb("sgate", [P, 2, 2, T])
        gmul = sb("gmul", [P, 2, 2, T])
        msum = sb("msum", [P, 2, T])

        at[0] = base
        act_hi = sb("act_hi", [P, FT, T], F32R)
        act_lo = sb("act_lo", [P, FT, T], F32R)
        x2 = sb("x2", [P, TT, D])
        sgf = sb("sgf", [P, 2, T])
        gact = sb("gact", [P, 2, T])
        prod = sb("prod", [P, 2, T])
        at[0] = base
        xn2 = sb("xn2", [P, TT, D])
        junk2 = sb("junk2", [P, D])
        at[0] = base
        zT = sb("zT", [P, KD, T])
        x3 = sb("x3", [P, TT, D])
        gfin = sb("gfin", [P, D])
        fin = sb("fin", [P, 2, D])
        junk3 = sb("junk3", [P, D])

        w_loaded = [sem(f"w_loaded{i}") for i in range(NRAW)]
        w_hi_ready = sem("w_hi_ready")
        w_lo_ready = sem("w_lo_ready")
        w_used = sem("w_used")
        prow_zero = sem("prow_zero")
        par_loaded = sem("par_loaded")
        x_loaded = [sem(f"x_loaded{i}") for i in range(TT)]
        lora_w_loaded = sem("lora_w_loaded")
        consts = sem("consts")
        par_T = sem("par_T")
        par_ready = sem("par_ready")
        omka_ready = sem("omka_ready")
        ss_ready = sem("ss_ready")
        ms_ready = sem("ms_ready")
        std_ready = sem("std_ready")
        rstd_ready = sem("rstd_ready")
        xn_ready = sem("xn_ready")
        xT_ready = sem("xT_ready")
        hhi_ready = sem("hhi_ready")
        hlo_ready = sem("hlo_ready")
        raw_ready = sem("raw_ready")
        rawd_ready = sem("rawd_ready")
        mixed_ready = sem("mixed_ready")
        lora_ready = sem("lora_ready")
        zeros_ready = sem("zeros_ready")
        pool_order = sem("pool_order")
        dve_order = sem("dve_order")
        kkf_sq = sem("kkf_sq")
        nrm2_mm = sem("nrm2_mm")
        nrm2_ready = sem("nrm2_ready")
        nrm_ready = sem("nrm_ready")
        rinv_ready = sem("rinv_ready")
        z_mm = sem("z_mm")
        za_mm = sem("za_mm")
        sg_ready = sem("sg_ready")
        a_ready = sem("a_ready")
        X_ready = sem("X_ready")
        gmid_ready = sem("gmid_ready")
        P_ready = sem("P_ready")
        E_ready = sem("E_ready")
        B_K_ready = sem("B_K_ready")
        kkE_R_ready = sem("kkE_R_ready")
        rk_ready = sem("rk_ready")
        gg_ready = sem("gg_ready")
        score_mm = sem("score_mm")
        score_ready = sem("score_ready")
        tok_mm = sem("tok_mm")
        tok_ready = sem("tok_ready")
        T_ident = sem("T_ident")
        T_first = sem("T_first")
        pr_mm = sem("pr_mm")
        pr_ready = sem("pr_ready")
        zz_mm = sem("zz_mm")
        T_ready = sem("T_ready")
        g_mm = sem("g_mm")
        G_ready = sem("G_ready")
        u_mm = sem("u_mm")
        U_ready = sem("U_ready")
        s_mm = sem("s_mm")
        S_ready = sem("S_ready")
        bonus_mm = sem("bonus_mm")
        bonv_ready = sem("bonv_ready")
        gate_mm = sem("gate_mm")
        gate_ready = sem("gate_ready")
        y_mm = sem("y_mm")
        yc_ready = sem("yc_ready")
        ysq_ready = sem("ysq_ready")
        yvar_ready = sem("yvar_ready")
        ystd_ready = sem("ystd_ready")
        yrstd_ready = sem("yrstd_ready")
        yn_ready = sem("yn_ready")
        yT_mm = sem("yT_mm")
        yT_ready = sem("yT_ready")
        ya_ready = sem("ya_ready")
        yahi_ready = sem("yahi_ready")
        yalo_ready = sem("yalo_ready")
        vb_ready = sem("vb_ready")
        fill_ready = sem("fill_ready")
        qk_stored = [sem(f"qk_stored{i}") for i in range(2)]
        qk_loaded = [sem(f"qk_loaded{i}") for i in range(NP_)]
        dist_ready = sem("dist_ready")
        alibi_ready = sem("alibi_ready")
        s_done = sem("s_done")
        sc_ready = sem("sc_ready")
        Pr_ready = sem("Pr_ready")
        pT_mm = sem("pT_mm")
        PT_ready = sem("PT_ready")
        pv_mm = sem("pv_mm")
        rrec_ready = sem("rrec_ready")
        O_ready = sem("O_ready")
        oT_mm = sem("oT_mm")
        obhi_ready = sem("obhi_ready")
        obf_ready = sem("obf_ready")
        oblo_ready = sem("oblo_ready")
        sgate_ready = sem("sgate_ready")
        gmul_ready = sem("gmul_ready")
        msum_ready = sem("msum_ready")
        mixhi_ready = sem("mixhi_ready")
        mixlo_ready = sem("mixlo_ready")
        x_again = sem("x_again")
        x2_ready = sem("x2_ready")
        sgf_ready = sem("sgf_ready")
        gact_ready = sem("gact_ready")
        prod_ready = sem("prod_ready")
        acthi_ready = sem("acthi_ready")
        actlo_ready = sem("actlo_ready")
        zT_ready = sem("zT_ready")
        z_T = sem("z_T")
        x3_ready = sem("x3_ready")
        gfin_loaded = sem("gfin_loaded")
        fin_ready = sem("fin_ready")
        out_done = [sem(f"out_done{i}") for i in range(2)]

        def pc(name, i=0, n=None):
            o, k = PC[name]
            return par[:, o + i:o + i + (k if n is None else n)]

        def wide(col, n=P):
            return col.unsqueeze(2).to_broadcast([P, col.shape[1], n])

        def first(t, b):
            return t.rearrange("p h (q two r) -> p h q two r", two=2, r=b)[:, :, :, 0, :]

        def second(t, b):
            return t.rearrange("p h (q two r) -> p h q two r", two=2, r=b)[:, :, :, 1, :]

        def unit_width(u):
            return KD * GH if isinstance(u, int) and u in (U_LORA + 1, U_LORA + 2) else 1024

        def shift_bank(u):
            return 4 + u % 2 if u else 0

        def cols(bank, shape, **k):
            return PS[:, bank, :].rearrange(shape, **k)

        block = ctx.enter_context(nc.Block())

        @block.sync
        def _(sp):
            def start_unit(u, fourth):
                slot = fourth % NRAW
                if not isinstance(u, int) or u >= NRAW:
                    sp.wait_ge(w_lo_ready, u - NRAW + 1)
                return slot

            def load_cols(u, fourth, w, c0, n=P, k0=0):
                slot = start_unit(u, fourth)
                dst = wraw[:, slot, 0:8 * n].rearrange("p (k c) -> p k c", k=8)
                src = w.rearrange("(k p) c -> p k c", p=P)
                for h in range(2):
                    sp.dma_start(dst[:, 4 * h:4 * h + 4, :], src[:, 4 * h:4 * h + 4, bass.ds(c0, n)])\
                      .then_inc(w_loaded[slot], 16)

            def load_rows(u, fourth, w, r0):
                slot = start_unit(u, fourth)
                for h in range(2):
                    sp.dma_start(wraw[:, slot, 512 * h:512 * h + 512],
                                 w[bass.ds(r0, P), 512 * h:512 * h + 512]).then_inc(w_loaded[slot], 16)

            for t in range(TT):
                sp.dma_start(xt[:, t, :], xd[:, t, :]).then_inc(x_loaded[t], 16)
            load_cols(U_LORA, U_LORA, w_in, C_WD)
            for h in range(2):
                load_cols(U_LORA + 1 + h, U_LORA + 1 + h, w_in, C_GD + GH * h, n=GH)
            load_cols(U_RKV, U_RKV, w_in, RKV_TILE[0] * P)
            sp.wait_ge(xT_ready, KD)
            sp.dma_start(wupda[0:HD, :], w_decay_up[0]).then_inc(lora_w_loaded, 16)
            sp.dma_start(wupda[HD:P, :], w_iclr_up[0]).then_inc(lora_w_loaded, 16)
            sp.dma_start(wupg[:], w_gate_up[0].rearrange("(h p) c -> p h c", p=GH)).then_inc(lora_w_loaded, 16)
            for j in range(1, 12):
                load_cols(U_RKV + j, U_RKV + j, w_in, RKV_TILE[j] * P)
            def store_qk(n):
                sp.wait_ge(fill_ready, n + 1)
                sp.dma_start(qk_dram[n].rearrange("p (a b) -> p a b", a=NP_), stage[:, n % 2, :, T - P:T])\
                  .then_inc(qk_stored[n % 2], 16)

            for n in range(2 * NP_):
                u = U_QK + n
                load_cols(u, u, w_in, (C_KB if n % 2 else C_Q) + P * (n // 2))
                if n >= 4:
                    store_qk(n - 4)
            for j in range(4):
                u = U_VB + j
                slot = start_unit(u, u)
                for h in range(2):
                    sp.dma_start(wraw[:, slot, 512 * h:512 * h + 512],
                                 w_in[(2 * j + h) * P:(2 * j + h + 1) * P, C_VB:C_VB + AW])\
                      .then_inc(w_loaded[slot], 16)
                store_qk(4 + j)
            sp.wait_ge(yalo_ready, TT)
            for i in range(2):
                sp.wait_ge(qk_stored[i], 16 * NP_)
            for p in range(NP_):
                sp.dma_start(qkT[:, 2 * p:2 * p + 2, :], qk_dram[2 * p:2 * p + 2].rearrange("n p t -> p n t"))\
                  .then_inc(qk_loaded[p], 16)
            for t in range(TT):
                sp.dma_start(x2[:, t, :], xd[:, t, :]).then_inc(x_again, 16)
            with sp.Fori(1, 3) as i1:
                for m in range(4):
                    u = U_GU - 12 + 12 * i1 + 3 * m
                    f = U_GU + 3 * m
                    load_cols(u, f, w_in, C_GA - 4 * P + (4 * i1 + m) * P)
                    load_cols(u + 1, f + 1, w_in, C_GB - 4 * P + (4 * i1 + m) * P)
                    slot = start_unit(u + 2, f + 2)
                    dst = wraw[:, slot, :].rearrange("p (k c) -> p k c", k=8)
                    for h, w in enumerate((w_up_a, w_up_b)):
                        sp.dma_start(dst[:, 4 * h:4 * h + 4, :],
                                     w.rearrange("(k p) c -> p k c", p=P)[:, :, bass.ds((4 * i1 + m - 4) * P, P)])\
                          .then_inc(w_loaded[slot], 16)
            for k in range(KD):
                load_rows(U_WO + k, U_WO + k, w_o, P * k)
            with sp.Fori(0, FT // 2) as i:
                for j in range(2):
                    u = U_FI + 4 * i + 2 * j
                    f = U_FI + 2 * j
                    load_cols(u, f, w_ffn_in, (2 * i + j) * P)
                    load_cols(u + 1, f + 1, w_ffn_in, F + (2 * i + j) * P)
            load_rows(U_FO, U_FO, w_ffn_out, 0)
            with sp.Fori(0, (FT - 2) // 4) as i:
                for j in range(4):
                    load_rows(U_FO + 1 + 4 * i + j, U_FO + 1 + j, w_ffn_out, (4 * i + 1 + j) * P)
            load_rows(U_FO + FT - 1, U_FO + FT - 1, w_ffn_out, (FT - 1) * P)
            sp.wait_ge(w_used, N_UNITS)
            sp.dma_start(gfin[:], norm_final_g.partition_broadcast(P)).then_inc(gfin_loaded, 16)
            for t in range(TT):
                sp.wait_ge(fin_ready, t + 1)
                sp.dma_start(outd[:, t, :], fin[:, t % 2, :]).then_inc(out_done[t % 2], 16)
            for i in range(2):
                sp.wait_ge(out_done[i], 16 * TT // 2)

        @block.gpsimd
        def _(pool):
            n = [0]

            def link(ins):
                n[0] += 1
                ins.then_inc(pool_order, 1)
                pool.wait_ge(pool_order, n[0])

            pool.memset(prow[:], 0.0).then_inc(prow_zero, 1)
            pool.wait_ge(prow_zero, 1)
            rows = ((mu_shift[0, 0:1536], "mu", P), (mu_shift[0, C_WD:C_WD + P], "mu_wa", P),
                    (mu_shift[0, C_GD:C_GD + GL], "mu_g", GH), (w0[0], "w0", P), (a0[0], "a0", P),
                    (k_k[0], "k_k", P), (k_a[0], "k_a", P), (r_k[0].rearrange("h d -> (h d)"), "r_k", P),
                    (ln_x_w[0], "ln_w", P), (ln_x_b[0], "ln_b", P), (norm_mix_g[0], "g_mix", P),
                    (norm_ffn_g[0], "g_ffn", P))
            for src, name, wdt in rows:
                o, k = PC[name]
                pool.dma_start(prow[o:o + k, 0:wdt], src.rearrange("(r c) -> r c", c=wdt)).then_inc(par_loaded, 16)

            link(pool.memset(tmpi[:], 1.0))
            link(pool.affine_select(out=ident[:], in_=tmpi[:], compare_op=ALU.is_equal, fill=0.0, base=0,
                                    pattern=[[-1, P]], channel_multiplier=1))
            link(pool.memset(blk1[:], 0.0))
            pool.memset(blk1[0:HD, 0:HD], 1.0)
            link(pool.memset(blk1[HD:P, HD:P], 1.0))
            pool.memset(ss[:, 2, :], 0.0).then_inc(consts, 1)
            pool.memset(raw[:, :, 0:1], 0.0).then_inc(zeros_ready, 1)
            pool.wait_ge(xT_ready, KD)
            pool.wait_ge(par_ready, 1)
            link(pool.memset(m_st[:], 1.0))
            link(pool.affine_select(out=m_st[:], in_=m_st[:], compare_op=ALU.is_ge, fill=0.0, base=-1,
                                    pattern=[[-1, P]], channel_multiplier=1))
            link(pool.memset(m_si[:], 1.0))
            for i in range(2):
                link(pool.affine_select(out=m_si[:, i, :], in_=m_si[:, i, :], compare_op=ALU.is_ge, fill=0.0,
                                        base=i - 1, pattern=[[1, P]], channel_multiplier=-1))
            link(pool.memset(resets[:], 1.0))
            link(pool.memset(resets[:].rearrange("p (a b) -> p a b", b=P)[:, :, 0:1], 0.0))
            link(pool.memset(lmask[:], -1.0))
            for li, b in enumerate([1] + LEVELS[:-1]):
                v = lmask[:, li, :].rearrange("p (q two r) -> p q two r", two=2, r=b)
                nq = HD // b
                f = v[:, :, 0, :]
                link(pool.affine_select(out=f, in_=f, compare_op=ALU.is_ge, fill=0.0, base=-b,
                                        pattern=[[-2 * b, nq], [0, b]], channel_multiplier=1))
                link(pool.affine_select(out=f, in_=f, compare_op=ALU.is_ge, fill=0.0, base=2 * b - 1,
                                        pattern=[[2 * b, nq], [0, b]], channel_multiplier=-1))
                link(pool.memset(v[:, :, 1, :], 0.0))
                link(pool.affine_select(out=lmask[:, li, :], in_=lmask[:, li, :], compare_op=ALU.not_equal, fill=1.0,
                                        base=0, pattern=[[-1, P]], channel_multiplier=1))
            for fill, base_ in ((-1.0, 0), (1.0, -1)):
                if fill < 0:
                    link(pool.memset(umask[:], 0.0))
                link(pool.affine_select(out=umask[:], in_=umask[:], compare_op=ALU.not_equal, fill=fill, base=base_,
                                        pattern=[[-2, HD]], channel_multiplier=1))
            for h in range(NH):
                pool.tensor_copy(M_ts[:, h, :], ident[:])
                pool.tensor_copy(MT_rb[:, h, 0, :], ident[:])
            pool.memset(MT_rb[:, :, 1, :], 0.0)
            pool.memset(LK_rk[:], 0.0).then_inc(zeros_ready, 1)

            def keys(c):
                kc = rkvT[:, 4:8, c * P:(c + 1) * P]
                if c:
                    pool.wait_ge(nrm2_mm, c)
                else:
                    pool.wait_ge(mixed_ready, U_RKV + 4)
                link(pool.tensor_tensor(kk[:], kc, wide(pc("k_k")), ALU.mult))
                pool.tensor_tensor(sq[:], kk[:], kk[:], ALU.mult).then_inc(kkf_sq, 1)

            def factors(c):
                par_ = c % 2
                cs = slice(c * P, (c + 1) * P)
                r_c, k_c = rkvT[:, 0:4, cs], rkvT[:, 4:8, cs]
                pool.wait_ge(a_ready, c + 1)
                link(pool.tensor_tensor(kp[:], aT[:], wide(pc("k_a")), ALU.mult))
                link(pool.tensor_tensor(kp[:], kp[:], wide(omka[:]), ALU.add))
                link(pool.tensor_tensor(kp[:], kp[:], k_c, ALU.mult))
                pool.wait_ge(X_ready, c + 1)
                link(pool.tensor_tensor(X[:], X[:], wide(x63[:]), ALU.subtract))
                pool.tensor_tensor(sg[:], X[:], sg[:], ALU.subtract).then_inc(P_ready, 1)
                pool.wait_ge(rinv_ready, c + 1)
                link(pool.tensor_tensor(kk[:], kk[:], rinv[:], ALU.mult))
                if c:
                    pool.wait_ge(tok_mm, 3 * c)
                    pool.wait_ge(score_mm, 10 * c)
                link(pool.tensor_tensor(Bt[:], kk[:], aT[:], ALU.mult))
                pool.wait_ge(E_ready, c + 1)
                pool.tensor_tensor(Bt[:], Bt[:], En[:], ALU.mult)
                pool.tensor_tensor(Kt[:], kp[:], En[:], ALU.mult).then_inc(B_K_ready, 1)
                if c >= 2:
                    pool.wait_ge(y_mm, c - 1)
                if c == 0:
                    pool.wait_ge(mixed_ready, U_RKV + 8)
                pool.tensor_tensor(kkE_R[:, par_, :, 0, :], kk[:], Ee[:], ALU.mult)
                pool.tensor_tensor(kkE_R[:, par_, :, 1, :], r_c, Ep[:], ALU.mult).then_inc(kkE_R_ready, 1)
                if c:
                    pool.wait_ge(bonus_mm, c)
                    pool.wait_ge(S_ready, c - 1) if c > 1 else None
                    pool.wait_ge(gmid_ready, c + 1)
                    link(pool.tensor_tensor(gg[:], gend[:], gmid[:], ALU.mult))
                    pool.tensor_copy(gend[:], Ep[:, :, P - 1]).then_inc(gg_ready, 1)
                else:
                    pool.tensor_copy(gend[:], Ep[:, :, P - 1])
                link(pool.tensor_tensor(rk[:], r_c, kp[:], ALU.mult))
                pool.tensor_tensor(rk[:], rk[:], wide(pc("r_k")), ALU.mult).then_inc(rk_ready, 1)

            def inverse_start(c):
                if c:
                    pool.wait_ge(u_mm, 2 * c)
                for h in range(NH):
                    pool.tensor_copy(second(Tm[:, h:h + 1, :], 1)[:, 0], ident[:].rearrange("p (q two) -> p q two", two=2)[:, :, 1:2])
                    ins = pool.tensor_copy(first(TmT[:, h:h + 1, :], 1)[:, 0], ident[:].rearrange("p (q two) -> p q two", two=2)[:, :, 0:1])
                ins.then_inc(T_ident, 1)

            def after_y(c):
                pool.wait_ge(yc_ready, c + 1)
                if c:
                    pool.wait_ge(yalo_ready, c)
                pool.tensor_tensor(ysq, yc[:], yc[:], ALU.mult).then_inc(ysq_ready, 1)

            def after_y2(c):
                pool.wait_ge(yrstd_ready, c + 1)
                pool.tensor_tensor(yT[:].rearrange("p i (two d) -> p two i d", two=2),
                                   yc[:].rearrange("p (two i) d -> p two i d", two=2),
                                   wide(yvar[:], HD).rearrange("p (two i) d -> p two i d", two=2),
                                   ALU.mult).then_inc(yn_ready, 1)

            def after_y3(c):
                pool.wait_ge(yT_ready, c + 1)
                pool.wait_ge(bonv_ready, c + 1)
                link(pool.tensor_tensor(yT[:], yT[:], bonv[:], ALU.add))
                pool.wait_ge(gate_ready, c + 1)
                pool.tensor_tensor(yT[:], yT[:], gsb[:], ALU.mult).then_inc(ya_ready, 1)

            keys(0)
            factors(0)
            inverse_start(0)
            for c in range(TT):
                if c + 1 < TT:
                    keys(c + 1)
                if c:
                    after_y3(c - 1)
                if c + 1 < TT:
                    factors(c + 1)
                after_y(c)
                if c + 1 < TT:
                    inverse_start(c + 1)
                after_y2(c)
            after_y3(TT - 1)

            pool.wait_ge(yahi_ready, TT)
            pool.wait_ge(yalo_ready, TT)
            link(pool.iota(dist[:].bitcast(mybir.dt.int32), pattern=[[-1, T]], base=T - P, channel_multiplier=1))
            link(pool.tensor_copy(sc[:, 0, :], dist[:].bitcast(mybir.dt.int32)))
            link(pool.affine_select(out=dist[:], in_=sc[:, 0, :], compare_op=ALU.is_ge, fill=BIG, base=T - P,
                                    pattern=[[-1, T]], channel_multiplier=1))
            pool.tensor_scalar(alibi[:, 0, :], dist[:], 0.5, None, ALU.mult).then_inc(alibi_ready, 1)
            pool.tensor_scalar(alibi[:, 1, :], dist[:], 0.25, None, ALU.mult).then_inc(alibi_ready, 1)
            for h in range(2, NH):
                pool.wait_ge(sc_ready, TT * (h - 1))
                pool.tensor_scalar(alibi[:, h % 2, :], alibi[:, h % 2, :], 0.25, None, ALU.mult)\
                    .then_inc(alibi_ready, 1)

            with pool.Fori(0, KD // 2) as i:
                for j in range(2):
                    pool.wait_ge(gmul_ready, 2 * i + j + 3)
                    pool.tensor_tensor(msum[:, j, :], gmul[:, j, 0, :], gmul[:, j, 1, :], ALU.add)\
                        .then_inc(msum_ready, 1)

        @block.scalar
        def _(act):
            def split_hi(u, fourth):
                s = fourth % NRAW
                act.wait_ge(w_loaded[s], (u - fourth % NRAW) // NRAW * 32 + 32 if isinstance(u, int)
                            else (u - s) * (32 // NRAW) + 32)
                if not isinstance(u, int) or u >= NSPL:
                    act.wait_ge(w_used, u - NSPL + 1)
                n = unit_width(u)
                act.activation(w_hi[:, fourth % NSPL, 0:n], wraw[:, s, 0:n], ACT.Copy).then_inc(w_hi_ready, 1)

            def squares(src, junk_, which, t, ready):
                act.wait_ge(*ready)
                if which or t:
                    act.wait_ge(ss_ready, which * TT + t)
                act.activation(junk_[:], src[:, t, :], ACT.Square, accum_out=ss[:, which, t:t + 1])\
                   .then_inc(ss_ready, 1)

            def std(k):
                act.wait_ge(ms_ready, k + 1)
                act.activation(rstd[:, k // TT, k % TT:k % TT + 1], ss[:, k // TT, k % TT:k % TT + 1], ACT.Sqrt)\
                   .then_inc(std_ready, 1)

            for t in range(TT):
                squares(xt, junk, 0, t, (x_loaded[t], 16))
            for t in range(TT):
                std(t)
            split_hi(0, 0)
            split_hi(1, 1)

            def h_hi(which, name):
                for k in range(KD):
                    act.wait_ge(xT_ready, which * KD + k + 1)
                    if which == 0 and k == 0:
                        act.wait_ge(par_ready, 1)
                    act.activation(hT_hi[:, k, :], PS[:, k, :], ACT.Copy, scale=pc(name, k, 1))\
                       .then_inc(hhi_ready, 1)

            h_hi(0, "g_mix")

            def raw_tile(u):
                act.wait_ge(w_used, u + 1)
                if u >= 2:
                    act.wait_ge(mixed_ready, u - 1)
                act.activation(raw[:, u % 2, 1:T + 1], PS[:, shift_bank(u), :], ACT.Copy).then_inc(raw_ready, 1)

            def lora_inputs():
                act.wait_ge(mixed_ready, U_LORA + 3)
                act.activation(loraT[0:HD, :], lmix[0:HD, 0, :], ACT.Tanh)
                act.activation(loraT[HD:P, :], lmix[HD:P, 0, :], ACT.Copy).then_inc(lora_ready, 1)
                act.activation(gdT[:], lmix[0:GH, 1:3, :], ACT.Sigmoid).then_inc(lora_ready, 1)

            def sigmoids(c):
                act.wait_ge(z_mm, c + 1)
                for p in range(NP_):
                    ins = act.activation(sg[:, p, :], cols(2, "p (a b) -> p a b", b=P)[:, p, :], ACT.Sigmoid,
                                         bias=pc("w0", p, 1))
                ins.then_inc(sg_ready, 1)
                act.wait_ge(za_mm, c + 1)
                if c:
                    act.wait_ge(B_K_ready, c)
                for p in range(NP_):
                    ins = act.activation(aT[:, p, :], cols(3, "p (a b) -> p a b", b=P)[:, p, :], ACT.Sigmoid,
                                         bias=pc("a0", p, 1))
                ins.then_inc(a_ready, 1)

            def exps(c):
                act.wait_ge(X_ready, c + 1)
                if c > 1:
                    act.wait_ge(gg_ready, c - 1)
                act.activation(gmid[:], x63[:], ACT.Exp, scale=-CDEC).then_inc(gmid_ready, 1)
                act.wait_ge(P_ready, c + 1)
                if c:
                    act.wait_ge(kkE_R_ready, c)
                    act.wait_ge(rk_ready, c)
                act.activation(Ep[:], X[:], ACT.Exp, scale=-CDEC)
                act.activation(En[:], X[:], ACT.Exp, scale=CDEC)
                act.activation(Ee[:], sg[:], ACT.Exp, scale=-CDEC).then_inc(E_ready, 1)

            def norms(c):
                act.wait_ge(nrm2_ready, c + 1)
                act.activation(rinv[:], rinv[:], ACT.Sqrt).then_inc(nrm_ready, 1)

            def tokens(c):
                for i, (dst, bank) in enumerate(((V_tok, 2), (B_tok, 3), (K_tok, 0))):
                    act.wait_ge(tok_mm, 3 * c + i + 1)
                    if c and i == 0:
                        act.wait_ge(s_mm, c)
                        act.wait_ge(y_mm, c)
                    act.activation(dst[:], PS[:, bank, :], ACT.Copy).then_inc(tok_ready, 1)

            def merge(c, li, half):
                b = LEVELS[li]
                k = 12 * c + 2 * li + half
                hs = slice(4 * half, 4 * half + 4)
                z = cols(6 + half, "p (k h q r) -> p k h q r", k=2, h=4, r=b)
                act.wait_ge(zz_mm, k + 1)
                if li < 5:
                    act.activation(first(Tm[:, hs, :], b), z[:, 0], ACT.Copy)
                    act.activation(second(TmT[:, hs, :], b), z[:, 1], ACT.Copy).then_inc(T_ready, 1)
                else:
                    act.activation(TmT[0:HD, hs, HD:P], PS[0:HD, 6 + half, 0:256].rearrange("p (h d) -> p h d", d=HD),
                                   ACT.Copy).then_inc(T_ready, 1)

            def minus_u(c):
                for half in range(2):
                    act.wait_ge(u_mm, 2 * c + half + 1)
                    if c:
                        act.wait_ge(s_mm, c)
                        act.wait_ge(y_mm, c)
                    act.activation(U_sb[:, 4 * half:4 * half + 4, :],
                                   PS[:, 6 + half, 0:256].rearrange("p (h d) -> p h d", d=HD), ACT.Copy,
                                   scale=-1.0).then_inc(U_ready, 1)

            def gate_out(c):
                act.wait_ge(gate_mm, c + 1)
                if c:
                    act.wait_ge(ya_ready, c)
                act.activation(gsb[:].rearrange("p a b -> p (a b)"), PS[:, 3, :], ACT.Copy).then_inc(gate_ready, 1)

            def ystd(c):
                act.wait_ge(yvar_ready, c + 1)
                act.activation(yvar[:], yvar[:], ACT.Sqrt).then_inc(ystd_ready, 1)

            def y_affine(c):
                act.wait_ge(yT_mm, c + 1)
                if c:
                    act.wait_ge(yalo_ready, c)
                for p in range(NP_):
                    ins = act.activation(yT[:, p, :], cols(1, "p (a b) -> p a b", b=P)[:, p, :], ACT.Identity,
                                         bias=pc("ln_b", p, 1), scale=pc("ln_w", p, 1))
                ins.then_inc(yT_ready, 1)

            def ya_hi(c):
                act.wait_ge(ya_ready, c + 1)
                if c == TT - 1:
                    for i in range(2):
                        act.wait_ge(qk_stored[i], 16 * NP_)
                act.activation(yaT_hi[:, :, c * P:(c + 1) * P], yT[:], ACT.Copy).then_inc(yahi_ready, 1)

            for u in range(N_SHIFT):
                split_hi(u + 2, u + 2)
                raw_tile(u)
                if u == 3:
                    lora_inputs()
                if u == 5:
                    sigmoids(0)
                if u == 9:
                    norms(0)
                if u == 11:
                    exps(0)
            def fill_out(n):
                act.wait_ge(w_used, U_QK + n + 1)
                if n >= 2:
                    act.wait_ge(qk_stored[n % 2], 16 * (n // 2))
                act.activation(stage[:, n % 2, :, T - P:T], cols(1, "p (a b) -> p a b", b=P), ACT.Copy,
                               scale=1.0 if n % 2 else -HD ** -0.5).then_inc(fill_ready, 1)

            for c in range(TT):
                more = c + 1 < TT
                if c:
                    split_hi(U_QK + 2 * c, U_QK + 2 * c)
                    split_hi(U_QK + 2 * c + 1, U_QK + 2 * c + 1)
                tokens(c)
                if c:
                    y_affine(c - 1)
                merge(c, 0, 0)
                merge(c, 0, 1)
                if more:
                    sigmoids(c + 1)
                merge(c, 1, 0)
                merge(c, 1, 1)
                if more:
                    norms(c + 1)
                merge(c, 2, 0)
                merge(c, 2, 1)
                if c:
                    ya_hi(c - 1)
                merge(c, 3, 0)
                merge(c, 3, 1)
                if more:
                    exps(c + 1)
                for li in range(4, 6):
                    merge(c, li, 0)
                    merge(c, li, 1)
                fill_out(2 * c)
                gate_out(c)
                minus_u(c)
                fill_out(2 * c + 1)
                if not more:
                    split_hi(U_VB, U_VB)
                    split_hi(U_VB + 1, U_VB + 1)
                ystd(c)
            split_hi(U_VB + 2, U_VB + 2)
            y_affine(TT - 1)
            split_hi(U_VB + 3, U_VB + 3)
            ya_hi(TT - 1)
            for j in range(2, 4):
                split_hi(U_VB + j + 2, U_VB + j + 2)

            act.wait_ge(yalo_ready, TT)
            act.wait_ge(w_used, U_VB + 4)
            for t in range(TT):
                act.activation(V_b[:, t, :], PS[:, VB_BANK[t], :], ACT.Copy).then_inc(vb_ready, 1)

            def probs(h, t):
                k = TT * h + t
                n = P * (t + 1)
                act.wait_ge(sc_ready, k + 1)
                if k >= 2:
                    act.wait_ge(pT_mm, k - 1)
                act.activation(Pr[:, k % 2, 0:n], sc[:, k % 2, 0:n], ACT.Exp, bias=nmax[:, h % 2, t:t + 1],
                               scale=-1.0, accum_out=rsum[:, h % 2, t:t + 1]).then_inc(Pr_ready, 1)

            def probs_T(k):
                n = P * (k % TT + 1)
                act.wait_ge(pT_mm, k + 1)
                if k >= 2:
                    act.wait_ge(pv_mm, k - 1)
                act.activation(PT[:, k % 2].rearrange("p a b -> p (a b)")[:, 0:n], PS[:, 4 + k % 2, 0:n], ACT.Copy)\
                   .then_inc(PT_ready, 1)

            def ob_hi(p):
                act.wait_ge(obf_ready, p + 1)
                act.activation(obT_hi[:, p, :], obf[:], ACT.Copy).then_inc(obhi_ready, 1)

            for p in range(NP_):
                for k in range(8 * p, 8 * p + 8):
                    probs(k // TT, k % TT)
                    if k >= 1:
                        probs_T(k - 1)
                    if k % 8 == 3 and p:
                        ob_hi(p - 1)
            probs_T(8 * NP_ - 1)
            ob_hi(NP_ - 1)

            act.wait_ge(oblo_ready, NP_)
            with act.Fori(0, 2) as i:
                for m in range(4):
                    u = U_GU + 12 * i + 3 * m
                    f = U_GU + 3 * m
                    b = 4 * (m % 2)
                    for g in range(2):
                        split_hi(u + 2 + g, f + 2 + g)
                        act.wait_ge(w_used, u + g + 1)
                        act.activation(sgate[:, m % 2, g, :], PS[:, b + g, :], ACT.Sigmoid)\
                           .then_inc(sgate_ready, 1)
                    split_hi(u + 4, f + 4)
                    act.wait_ge(msum_ready, 4 * i + m + 1)
                    act.activation(mixT_hi[:, bass.ds(4 * i + m, 1), :], msum[:, m % 2:m % 2 + 1, :], ACT.Copy)\
                       .then_inc(mixhi_ready, 1)

            for k in range(KD):
                split_hi(U_WO + k + 2, U_WO + k + 2)
            for t in range(TT):
                squares(x2, junk2, 1, t, (x2_ready, t + 1))
                std(TT + t)
            h_hi(1, "g_ffn")

            with act.Fori(0, FT // 2) as i:
                for j in range(2):
                    u = U_FI + 4 * i + 2 * j
                    f = U_FI + 2 * j
                    split_hi(u + 2, f + 2)
                    act.wait_ge(w_used, u + 1)
                    act.activation(sgf[:, j, :], PS[:, 2 * j, :], ACT.Sigmoid).then_inc(sgf_ready, 1)
                    split_hi(u + 3, f + 3)
                    act.wait_ge(prod_ready, 2 * i + j + 3)
                    act.activation(act_hi[:, bass.ds(2 * i + j, 1), :], prod[:, j:j + 1, :], ACT.Copy)\
                       .then_inc(acthi_ready, 1)

            with act.Fori(0, (FT - 2) // 4) as i:
                for j in range(4):
                    split_hi(U_FO + 2 + 4 * i + j, U_FO + 2 + j)
            act.wait_ge(w_used, N_UNITS)
            for m in range(1, KD, 2):
                act.activation(zT[:, m, :], PS[:, m, :], ACT.Copy).then_inc(zT_ready, 1)
            for t in range(TT):
                squares(x3, junk3, 2, t, (x3_ready, t + 1))
                std(2 * TT + t)

        @block.vector
        def _(dve):
            n = [0]

            def link(ins):
                n[0] += 1
                ins.then_inc(dve_order, 1)
                dve.wait_ge(dve_order, n[0])

            def split_lo(u, fourth):
                s, q = fourth % NRAW, fourth % NSPL
                dve.wait_ge(w_hi_ready, u + 1)
                n = unit_width(u)
                dve.tensor_tensor(w_lo[:, q, 0:n], wraw[:, s, 0:n], w_hi[:, q, 0:n].bitcast(F32), ALU.subtract)\
                   .then_inc(w_lo_ready, 1)

            def mean_square(which, t):
                k = which * TT + t
                dve.wait_ge(ss_ready, k + 1)
                s = ss[:, which, t:t + 1]
                dve.tensor_scalar(s, s, 1.0 / D, RMS_EPS, ALU.mult, ALU.add).then_inc(ms_ready, 1)

            def norm(src, dst, which, t):
                k = which * TT + t
                dve.wait_ge(std_ready, k + 1)
                r = rstd[:, which, t:t + 1]
                dve.reciprocal(r, r).then_inc(rstd_ready, 1)
                dve.wait_ge(rstd_ready, k + 1)
                if dst is not None:
                    dve.tensor_scalar(dst[:, t, :], src[:, t, :], r, None, ALU.mult).then_inc(xn_ready, 1)

            def h_lo(which, name):
                for k in range(KD):
                    dve.wait_ge(hhi_ready, which * KD + k + 1)
                    dve.scalar_tensor_tensor(out=hT_lo[:, k, :], in0=PS[:, k, :], scalar=pc(name, k, 1),
                                             in1=hT_hi[:, k, :].bitcast(F32), op0=ALU.mult, op1=ALU.subtract)\
                       .then_inc(hlo_ready, 1)

            dve.wait_ge(par_T, 1)
            dve.tensor_copy(par[:], PS[:, 7, 0:NPAR]).then_inc(par_ready, 1)
            dve.wait_ge(par_ready, 1)
            dve.tensor_scalar(omka[:], pc("k_a"), -1.0, 1.0, ALU.mult, ALU.add).then_inc(omka_ready, 1)
            for t in range(TT):
                mean_square(0, t)
            for t in range(TT):
                norm(xt, xn, 0, t)
            split_lo(0, 0)
            split_lo(1, 1)
            h_lo(0, "g_mix")

            def shift(u):
                np_, j = P, u % 2
                if u == U_LORA:
                    dst, mu = lmix[:, 0, :], pc("mu_wa")
                elif u < U_RKV:
                    np_ = GH
                    dst, mu = lmix[0:GH, u, :], par[0:GH, PC["mu_g"][0] + u - 1:PC["mu_g"][0] + u]
                else:
                    tile = RKV_TILE[u - U_RKV]
                    dst, mu = rkvT[:, tile, :], pc("mu", tile, 1)
                dve.wait_ge(raw_ready, u + 1)
                dve.tensor_tensor(rawd[0:np_, j, :], raw[0:np_, j, 0:T], raw[0:np_, j, 1:T + 1], ALU.subtract)\
                   .then_inc(rawd_ready, 1)
                dve.wait_ge(rawd_ready, u + 1)
                dve.scalar_tensor_tensor(out=dst, in0=rawd[0:np_, j, :], scalar=mu, in1=raw[0:np_, j, 1:T + 1],
                                         op0=ALU.mult, op1=ALU.add).then_inc(mixed_ready, 1)

            def key_norm(c):
                dve.wait_ge(nrm2_mm, c + 1)
                dve.tensor_scalar(rinv[:], cols(0, "p (a b) -> p a b", b=P), 1e-24, None, ALU.max)\
                   .then_inc(nrm2_ready, 1)

            def key_norm2(c):
                dve.wait_ge(nrm_ready, c + 1)
                dve.reciprocal(rinv[:], rinv[:]).then_inc(rinv_ready, 1)

            def decay_sums(c):
                dve.wait_ge(sg_ready, c + 1)
                if c:
                    dve.wait_ge(E_ready, c)
                link(dve.tensor_tensor_scan(X[:].rearrange("p a b -> p (a b)"), resets[:],
                                            sg[:].rearrange("p a b -> p (a b)"), 0.0, ALU.mult, ALU.add))
                if c:
                    dve.wait_ge(gmid_ready, c)
                dve.tensor_copy(x63[:], X[:, :, HD - 1]).then_inc(X_ready, 1)

            def scores(c):
                for q in range(10):
                    dve.wait_ge(score_mm, 10 * c + q + 1)
                    if c and q == 0:
                        dve.wait_ge(y_mm, c)
                    odd = q % 2
                    if q < 2:
                        dst = M_ts[:, 4 * odd:4 * odd + 4, :]
                        mask = m_st[:].unsqueeze(1).to_broadcast([P, 4, P])
                        src = cols(q % 4, "p (h t) -> p h t", h=4)
                    else:
                        h = 4 * odd + 2 * ((q - 2) % 4 // 2)
                        dst = (MT_rb if q < 6 else LK_rk)[:, h:h + 2]
                        mask = m_si[:].unsqueeze(1).to_broadcast([P, 2, 2, P])
                        src = cols(q % 4, "p (h k t) -> p h k t", h=2, k=2)
                    dve.copy_predicated(out=dst, mask=mask.bitcast(U32), data=src).then_inc(score_ready, 1)

            def first_merge(c):
                dve.wait_ge(T_ident, c + 1)
                dve.wait_ge(score_ready, 10 * c + 6)
                for half in range(2):
                    hs = slice(4 * half, 4 * half + 4)
                    dve.tensor_tensor(first(Tm[:, hs, :], 1), first(M_ts[:, hs, :], 1),
                                      lmask[:, 0, 0:P:2].unsqueeze(1).unsqueeze(3).to_broadcast([P, 4, HD, 1]),
                                      ALU.mult)
                    dve.tensor_tensor(second(TmT[:, hs, :], 1), second(MT_rb[:, hs, 0, :], 1),
                                      umask[:].unsqueeze(1).unsqueeze(3).to_broadcast([P, 4, HD, 1]), ALU.mult)\
                       .then_inc(T_first, 1)

            def merge(c, li, half):
                k = 12 * c + 2 * li + half
                dve.wait_ge(pr_mm, k + 1)
                w = cols(4 + half, "p (h c) -> p h c", h=4)
                if li < 5:
                    dve.tensor_tensor(PR[:, half], w, lmask[:, li + 1, :].unsqueeze(1).to_broadcast([P, 4, P]),
                                      ALU.mult).then_inc(pr_ready, 1)
                else:
                    dve.tensor_scalar(PR[HD:P, half, :, 0:HD], w[HD:P, :, 0:HD], -1.0, None, ALU.mult)\
                       .then_inc(pr_ready, 1)

            def state_g(c):
                for half in range(2):
                    dve.wait_ge(g_mm, 2 * c + half + 1)
                    dve.tensor_copy(G_sb[:, 4 * half:4 * half + 4, :],
                                    PS[:, 4 + half, 0:256].rearrange("p (h d) -> p h d", d=HD)).then_inc(G_ready, 1)

            def bonus(c):
                dve.wait_ge(bonus_mm, c + 1)
                if c:
                    dve.wait_ge(ya_ready, c)
                dve.tensor_tensor(bonv[:], cols(2, "p (a b) -> p a b", b=P), rkvT[:, 8:12, c * P:(c + 1) * P],
                                  ALU.mult).then_inc(bonv_ready, 1)

            def state(c):
                src = PS[:, 0, 0:256].rearrange("p (a d) -> p a d", d=HD)
                dve.wait_ge(s_mm, c + 1)
                dve.wait_ge(gg_ready, c + 1)
                if c:
                    link(dve.tensor_tensor(S_tmp[:], src, S_sb[:], ALU.add))
                    dve.wait_ge(y_mm, c + 1)
                    dve.tensor_tensor(S_sb[:], S_tmp[:], wide(gg[:], HD), ALU.mult).then_inc(S_ready, 1)
                else:
                    dve.tensor_tensor(S_sb[:], src, wide(gg[:], HD), ALU.mult).then_inc(S_ready, 1)

            def y_centre(c):
                y = PS[:, 1:5:3, 0:256]
                dve.wait_ge(y_mm, c + 1)
                link(dve.tensor_reduce(ysum[:].rearrange("p (a b) -> p a b", a=2),
                                       y.rearrange("p a (b d) -> p a b d", d=HD), AX.X, ALU.add))
                if c:
                    dve.wait_ge(yT_mm, c)
                dve.scalar_tensor_tensor(out=yc[:].rearrange("p (a b) d -> p a b d", a=2),
                                         in0=wide(ysum[:], HD).rearrange("p (a b) d -> p a b d", a=2),
                                         scalar=-1.0 / HD, in1=y.rearrange("p a (b d) -> p a b d", d=HD),
                                         op0=ALU.mult, op1=ALU.add).then_inc(yc_ready, 1)

            def y_var(c):
                dve.wait_ge(ysq_ready, c + 1)
                link(dve.tensor_reduce(yvar[:], ysq, AX.X, ALU.add))
                dve.tensor_scalar(yvar[:], yvar[:], 1.0 / HD, GN_EPS, ALU.mult, ALU.add).then_inc(yvar_ready, 1)

            def y_rstd(c):
                dve.wait_ge(ystd_ready, c + 1)
                dve.reciprocal(yvar[:], yvar[:]).then_inc(yrstd_ready, 1)

            def ya_lo(c):
                cs = slice(c * P, (c + 1) * P)
                dve.wait_ge(yahi_ready, c + 1)
                dve.tensor_tensor(yaT_lo[:, :, cs], yT[:], yaT_hi[:, :, cs].bitcast(F32), ALU.subtract)\
                   .then_inc(yalo_ready, 1)

            dve.wait_ge(zeros_ready, 1)
            for u in range(N_SHIFT):
                split_lo(u + 2, u + 2)
                shift(u)
                if u == 6:
                    dve.wait_ge(zeros_ready, 2)
                    decay_sums(0)
                if u == 9:
                    key_norm(0)
                if u == 10:
                    key_norm2(0)
            for c in range(TT):
                more = c + 1 < TT
                if c:
                    split_lo(U_QK + 2 * c, U_QK + 2 * c)
                    split_lo(U_QK + 2 * c + 1, U_QK + 2 * c + 1)
                scores(c)
                first_merge(c)
                merge(c, 0, 0)
                merge(c, 0, 1)
                merge(c, 1, 0)
                merge(c, 1, 1)
                if more:
                    key_norm(c + 1)
                    decay_sums(c + 1)
                merge(c, 2, 0)
                merge(c, 2, 1)
                if more:
                    key_norm2(c + 1)
                merge(c, 3, 0)
                merge(c, 3, 1)
                if c:
                    ya_lo(c - 1)
                for li in range(4, 6):
                    merge(c, li, 0)
                    merge(c, li, 1)
                state_g(c)
                bonus(c)
                if more:
                    state(c)
                y_centre(c)
                y_var(c)
                if not more:
                    split_lo(U_VB, U_VB)
                    split_lo(U_VB + 1, U_VB + 1)
                y_rstd(c)
            split_lo(U_VB + 2, U_VB + 2)
            split_lo(U_VB + 3, U_VB + 3)
            ya_lo(TT - 1)

            for j in range(2, 4):
                split_lo(U_VB + j + 2, U_VB + j + 2)

            def score_bias(h, t):
                k = TT * h + t
                w = P * (t + 1)
                dve.wait_ge(s_done, k + 1)
                dve.wait_ge(alibi_ready, h + 1)
                if k >= 2:
                    dve.wait_ge(Pr_ready, k - 1)
                dve.tensor_tensor_reduce(sc[:, k % 2, 0:w], PS[:, 2 + k % 2, 0:w], alibi[:, h % 2, T - w:T],
                                         1.0, 3e38, ALU.add, ALU.min, nmax[:, h % 2, t:t + 1]).then_inc(sc_ready, 1)

            def attn_out(h):
                dve.wait_ge(Pr_ready, TT * (h + 1))
                dve.reciprocal(rrec[:, h % 2, :], rsum[:, h % 2, :]).then_inc(rrec_ready, 1)
                dve.wait_ge(rrec_ready, h + 1)
                dve.wait_ge(pv_mm, TT * (h + 1))
                if h >= 2 and h % 2 == 0:
                    dve.wait_ge(oT_mm, h // 2)
                dve.tensor_tensor(O_sb[:, :, HD * (h % 2):HD * (h % 2) + HD],
                                  PS[:, 6, 0:256].rearrange("p (t d) -> p t d", d=HD), wide(rrec[:, h % 2, :], HD),
                                  ALU.mult).then_inc(O_ready, 1)

            def ob_lo(p):
                dve.wait_ge(obhi_ready, p + 1)
                dve.tensor_tensor(obT_lo[:, p, :], obf[:], obT_hi[:, p, :].bitcast(F32), ALU.subtract)\
                   .then_inc(oblo_ready, 1)

            def ob_copy(p):
                dve.wait_ge(oT_mm, p + 1)
                dve.tensor_copy(obf[:], PS[:, 7, :]).then_inc(obf_ready, 1)

            for h in range(NH):
                p = h // 2
                for t in range(TT):
                    score_bias(h, t)
                    if t == 1 and h:
                        attn_out(h - 1)
                    if t == 3 and h % 2 == 0 and p:
                        ob_copy(p - 1)
                if h % 2 == 1 and p:
                    ob_lo(p - 1)
            attn_out(NH - 1)
            ob_copy(NP_ - 1)
            ob_lo(NP_ - 1)

            dve.memset(ss[:, 0, 0:1], 0.0).then_inc(gmul_ready, 2)
            with dve.Fori(0, 2) as i:
                for m in range(4):
                    u = U_GU + 12 * i + 3 * m
                    f = U_GU + 3 * m
                    b = 4 * (m % 2)
                    k = 4 * i + m
                    for g in range(3):
                        split_lo(u + 2 + g, f + 2 + g)
                    dve.wait_ge(sgate_ready, 2 * k + 2)
                    dve.wait_ge(w_used, u + 3)
                    dve.tensor_tensor(gmul[:, m % 2], sgate[:, m % 2], PS[:, b + 2:b + 4, :], ALU.mult)\
                       .then_inc(gmul_ready, 1)
                    dve.wait_ge(mixhi_ready, k + 1)
                    dve.tensor_tensor(mixT_lo[:, bass.ds(k, 1), :], msum[:, m % 2:m % 2 + 1, :],
                                      mixT_hi[:, bass.ds(k, 1), :].bitcast(F32), ALU.subtract)\
                       .then_inc(mixlo_ready, 1)

            for k in range(KD):
                split_lo(U_WO + k + 2, U_WO + k + 2)
            dve.memset(ss[:, 0, 0:1], 0.0).then_inc(prod_ready, 2)
            dve.wait_ge(x_again, 16 * TT)
            dve.wait_ge(w_used, U_WO + KD)
            for t in range(TT):
                dve.tensor_tensor(x2[:, t, :].rearrange("p (a b) -> p a b", a=2),
                                  x2[:, t, :].rearrange("p (a b) -> p a b", a=2), PS[:, 2 * t:2 * t + 2, :],
                                  ALU.add).then_inc(x2_ready, 1)
            for t in range(TT):
                mean_square(1, t)
                norm(x2, xn2, 1, t)
            h_lo(1, "g_ffn")

            with dve.Fori(0, FT // 2) as i:
                for j in range(2):
                    u = U_FI + 4 * i + 2 * j
                    f = U_FI + 2 * j
                    k = 2 * i + j
                    split_lo(u + 2, f + 2)
                    dve.wait_ge(sgf_ready, k + 1)
                    dve.tensor_tensor(gact[:, j, :], sgf[:, j, :], PS[:, 2 * j, :], ALU.mult).then_inc(gact_ready, 1)
                    split_lo(u + 3, f + 3)
                    dve.wait_ge(gact_ready, k + 1)
                    dve.wait_ge(w_used, u + 2)
                    dve.tensor_tensor(prod[:, j, :], gact[:, j, :], PS[:, 2 * j + 1, :], ALU.mult)\
                       .then_inc(prod_ready, 1)
                    dve.wait_ge(acthi_ready, k + 1)
                    dve.tensor_tensor(act_lo[:, bass.ds(k, 1), :], prod[:, j:j + 1, :],
                                      act_hi[:, bass.ds(k, 1), :].bitcast(F32), ALU.subtract)\
                       .then_inc(actlo_ready, 1)

            with dve.Fori(0, (FT - 2) // 4) as i:
                for j in range(4):
                    split_lo(U_FO + 2 + 4 * i + j, U_FO + 2 + j)
            dve.wait_ge(w_used, N_UNITS)
            for m in range(0, KD, 2):
                dve.tensor_copy(zT[:, m, :], PS[:, m, :]).then_inc(zT_ready, 1)
            for t in range(TT):
                dve.wait_ge(z_T, t + 1)
                dve.tensor_tensor(x3[:, t, :].rearrange("p (a b) -> p a b", a=2),
                                  x2[:, t, :].rearrange("p (a b) -> p a b", a=2), PS[:, 2 * t:2 * t + 2, :],
                                  ALU.add).then_inc(x3_ready, 1)
                mean_square(2, t)
            dve.wait_ge(gfin_loaded, 16)
            for t in range(TT):
                norm(None, None, 2, t)
                if t >= 2:
                    dve.wait_ge(out_done[t % 2], 16 * (t // 2))
                dve.scalar_tensor_tensor(out=fin[:, t % 2, :], in0=x3[:, t, :], scalar=rstd[:, 2, t:t + 1],
                                         in1=gfin[:], op0=ALU.mult, op1=ALU.mult).then_inc(fin_ready, 1)

        @block.tensor
        def _(pe):
            def three(out_, a_hi, a_lo, b_hi, b_lo, start, stop):
                pe.matmul(out_, a_hi, b_hi, start=start, stop=False)
                pe.matmul(out_, a_hi, b_lo, start=False, stop=False)
                return pe.matmul(out_, a_lo, b_hi, start=False, stop=stop)

            def project(u, fourth, bank, width=P, act_=(hT_hi, hT_lo), k0=0, nk=KD, fresh=None):
                q = fourth % NSPL
                for k in range(nk):
                    if fresh is not None:
                        pe.wait_ge(hlo_ready, fresh + k + 1)
                    w = slice((k0 + k) * width, (k0 + k + 1) * width)
                    ins = three(PS[0:width, bank, :], w_hi[:, q, w], w_lo[:, q, w], act_[0][:, k, :],
                                act_[1][:, k, :], k == 0, k == nk - 1)
                return ins

            def take(u):
                pe.wait_ge(w_lo_ready, u + 1)

            def transposes(which, src):
                for t in range(TT):
                    pe.wait_ge(xn_ready, which * TT + t + 1)
                    for k in range(KD):
                        ins = pe.transpose(PS[:, k, t * P:(t + 1) * P], src[:, t, k * P:(k + 1) * P], ident[:])
                        if t == TT - 1:
                            ins.then_inc(xT_ready, 1)

            pe.wait_ge(consts, 1)
            pe.wait_ge(par_loaded, 16 * 12)
            pe.transpose(PS[:, 7, 0:NPAR], prow[0:NPAR, :], ident[0:NPAR, 0:NPAR]).then_inc(par_T, 1)
            pe.wait_ge(par_ready, 1)
            transposes(0, xn)

            def lora(c):
                cs = slice(c * P, (c + 1) * P)
                if c:
                    pe.wait_ge(tok_ready, 3 * c)
                else:
                    pe.wait_ge(lora_ready, 2)
                    pe.wait_ge(lora_w_loaded, 48)
                for p in range(NP_):
                    ins = pe.matmul(PS[:, 2, p * P:(p + 1) * P], wupda[0:HD, p * P:(p + 1) * P], loraT[0:HD, cs],
                                    start=True, stop=True)
                ins.then_inc(z_mm, 1)
                for p in range(NP_):
                    ins = pe.matmul(PS[:, 3, p * P:(p + 1) * P], wupda[HD:P, p * P:(p + 1) * P], loraT[HD:P, cs],
                                    start=True, stop=True)
                ins.then_inc(za_mm, 1)

            def key_norm(c):
                pe.wait_ge(kkf_sq, c + 1)
                pe.matmul(PS[:, 0, :], blk1[:], sq[:].rearrange("p a b -> p (a b)"), start=True, stop=True)\
                  .then_inc(nrm2_mm, 1)

            def scores(c):
                par_ = c % 2
                pe.wait_ge(B_K_ready, c + 1)
                pe.wait_ge(kkE_R_ready, c + 1)
                def bank_free(q):
                    if q >= 4:
                        pe.wait_ge(score_ready, 10 * c + q - 3)
                    elif c:
                        pe.wait_ge(*((S_ready, c), (yc_ready, c), (bonv_ready, c), (gate_ready, c))[q])
                    else:
                        pe.wait_ge(*((nrm2_ready, 1), (hlo_ready, KD), (sg_ready, 1), (a_ready, 1))[q])

                for q in range(0, 10, 2):
                    bank_free(q)
                    bank_free(q + 1)
                    for i in range(4 if q < 2 else 2):
                        for odd in range(2):
                            r = slice(HD * odd, HD * odd + HD)
                            if q < 2:
                                ins = pe.matmul(PS[:, odd, i * P:(i + 1) * P], kkE_R[r, par_, i, 0, :],
                                                Bt[r, i, :], start=True, stop=True)
                            else:
                                p = 2 * ((q - 2) % 4 // 2) + i
                                ins = pe.matmul(PS[:, (q + odd) % 4, i * 2 * P:(i + 1) * 2 * P],
                                                (Bt if q < 6 else Kt)[r, p, :],
                                                kkE_R[r, par_, p, :, :].rearrange("p a b -> p (a b)"),
                                                start=True, stop=True)
                            if i == (3 if q < 2 else 1):
                                ins.then_inc(score_mm, 1)

            def tokens(c):
                cs = slice(c * P, (c + 1) * P)
                for i, (bank, sd) in enumerate(((2, 7), (3, 8), (0, 9))):
                    pe.wait_ge(score_ready, 10 * c + sd)
                    for p in range(NP_):
                        src = (rkvT[:, 8 + p, cs], Bt[:, p, :], Kt[:, p, :])[i]
                        ins = pe.transpose(PS[:, bank, p * P:(p + 1) * P], src, ident[:])
                    ins.then_inc(tok_mm, 1)

            def products(c, li, half):
                k = 12 * c + 2 * li + half
                if li:
                    pe.wait_ge(T_ready, k - 1)
                else:
                    pe.wait_ge(T_first, 2 * c + half + 1)
                    if c and half == 0:
                        pe.wait_ge(yc_ready, c)
                    if c:
                        pe.wait_ge(G_ready, 2 * (c - 1) + half + 1)
                for i in range(4):
                    h = 4 * half + i
                    if li < 5:
                        ins = pe.matmul(PS[:, 4 + half, i * P:(i + 1) * P], MT_rb[:, h, 0, :], Tm[:, h, :],
                                        start=True, stop=True)
                    else:
                        ins = pe.matmul(PS[HD:P, 4 + half, i * P:i * P + HD], MT_rb[0:HD, h, 0, HD:P],
                                        Tm[0:HD, h, 0:HD], start=True, stop=True)
                ins.then_inc(pr_mm, 1)

            def merge(c, li, half):
                b = LEVELS[li]
                k = 12 * c + 2 * li + half
                pe.wait_ge(pr_ready, k + 1)
                if li == 0 and c:
                    pe.wait_ge(U_ready, 2 * (c - 1) + half + 1)
                for i in range(4):
                    h = 4 * half + i
                    w = PR[:, half, i:i + 1, :]
                    if li < 5:
                        pe.matmul(PS[:, 6 + half, i * HD:(i + 1) * HD], TmT[:, h, :], first(w, b)[:, 0],
                                  start=True, stop=True)
                        ins = pe.matmul(PS[:, 6 + half, 256 + i * HD:256 + (i + 1) * HD], PR[:, half, i, :],
                                        second(TmT[:, h:h + 1, :], b)[:, 0], start=True, stop=True)
                    else:
                        ins = pe.matmul(PS[0:HD, 6 + half, i * HD:(i + 1) * HD], PR[HD:P, half, i, 0:HD],
                                        TmT[HD:P, h, HD:P], start=True, stop=True)
                ins.then_inc(zz_mm, 1)

            def fill(c, i, k0, nk):
                u = U_QK + 2 * c + i
                q = u % NSPL
                for k in range(k0, k0 + nk):
                    if k == 0:
                        take(u)
                        if c or i:
                            pe.wait_ge(*((fill_ready, 2 * c + 1) if i else (yT_ready, c)))
                    w = slice(k * P, (k + 1) * P)
                    ins = three(PS[:, 1, :], w_hi[:, q, w], w_lo[:, q, w], hT_hi[:, k, :], hT_lo[:, k, :], k == 0,
                                k == KD - 1)
                if k == KD - 1:
                    ins.then_inc(w_used, 1)

            def solve(c):
                par_ = c % 2
                pe.wait_ge(tok_ready, 3 * c + 3)
                pe.wait_ge(score_ready, 10 * c + 10)
                if c:
                    pe.wait_ge(S_ready, c)
                pe.wait_ge(pr_ready, 12 * (c + 1))
                for odd in range(2):
                    r = slice(HD * odd, HD * odd + HD)
                    for i in range(4):
                        h = 2 * i + odd
                        o = PS[:, 4 + odd, i * HD:(i + 1) * HD]
                        ins = pe.matmul(o, LK_rk[:, 4 * odd + i, 0, :], V_tok[:, h * HD:(h + 1) * HD], start=True,
                                        stop=c == 0)
                        if c:
                            ins = pe.matmul(o, kkE_R[r, par_, i, 0, :], S_sb[r, i, :], start=False, stop=True)
                    ins.then_inc(g_mm, 1)
                pe.wait_ge(rk_ready, c + 1)
                pe.wait_ge(sg_ready, min(c + 2, TT))
                pe.matmul(PS[:, 2, :], blk1[:], rk[:].rearrange("p a b -> p (a b)"), start=True, stop=True)\
                  .then_inc(bonus_mm, 1)
                pe.wait_ge(a_ready, min(c + 2, TT))
                for p in range(NP_):
                    for k in range(2):
                        ins = pe.matmul(PS[:, 3, p * P:(p + 1) * P], wupg[:, k, p * P:(p + 1) * P],
                                        gdT[:, k, c * P:(c + 1) * P], start=k == 0, stop=k == 1)
                ins.then_inc(gate_mm, 1)
                fill(c, 1, 0, 2)
                for half in range(2):
                    pe.wait_ge(G_ready, 2 * c + half + 1)
                    pe.wait_ge(T_ready, 12 * (c + 1))
                    for i in range(4):
                        h = 4 * half + i
                        ins = pe.matmul(PS[:, 6 + half, i * HD:(i + 1) * HD], TmT[:, h, :], G_sb[:, h, :],
                                        start=True, stop=True)
                    ins.then_inc(u_mm, 1)

            def state(c):
                pe.wait_ge(U_ready, 2 * c + 2)
                if c + 1 < TT:
                    pe.wait_ge(nrm2_ready, c + 2)
                for h in range(NH):
                    r = slice(HD * (h % 2), HD * (h % 2) + HD)
                    hc = slice(h * HD, (h + 1) * HD)
                    o = PS[r, 0, (h // 2) * HD:(h // 2 + 1) * HD]
                    pe.matmul(o, K_tok[:, hc], V_tok[:, hc], start=True, stop=False)
                    ins = pe.matmul(o, B_tok[:, hc], U_sb[:, 4 * (h % 2) + h // 2, :], start=False, stop=True)
                ins.then_inc(s_mm, 1)

            def outputs(c):
                par_ = c % 2
                pe.wait_ge(U_ready, 2 * c + 2)
                pe.wait_ge(G_ready, 2 * c + 1)
                for odd, bank in ((1, 4), (0, 1)):
                    if bank == 1:
                        pe.wait_ge(fill_ready, 2 * c + 2)
                    r = slice(HD * odd, HD * odd + HD)
                    for i in range(4):
                        h, sh = 2 * i + odd, 4 * odd + i
                        o = PS[:, bank, i * HD:(i + 1) * HD]
                        pe.matmul(o, LK_rk[:, sh, 1, :], V_tok[:, h * HD:(h + 1) * HD], start=True, stop=False)
                        ins = pe.matmul(o, MT_rb[:, sh, 1, :], U_sb[:, sh, :], start=False, stop=c == 0)
                        if c:
                            ins = pe.matmul(o, kkE_R[r, par_, i, 1, :], S_sb[r, i, :], start=False, stop=True)
                ins.then_inc(y_mm, 1)

            def y_T(c):
                pe.wait_ge(yn_ready, c + 1)
                if c + 1 < TT:
                    pe.wait_ge(score_ready, 10 * (c + 1) + 10)
                for p in range(NP_):
                    ins = pe.transpose(PS[:, 1, p * P:(p + 1) * P],
                                       yT[:, p, :], ident[:])
                ins.then_inc(yT_mm, 1)

            for u in range(N_SHIFT):
                take(u)
                if u >= 3:
                    pe.wait_ge(raw_ready, u - 1)
                project(u, u, shift_bank(u), GH if u in (U_LORA + 1, U_LORA + 2) else P, fresh=0 if u == 0 else None)\
                    .then_inc(w_used, 1)
                if u == 4:
                    lora(0)
                if u == 8:
                    key_norm(0)
            pe.wait_ge(raw_ready, N_SHIFT)
            pe.wait_ge(mixed_ready, N_SHIFT)
            pe.wait_ge(zeros_ready, 2)
            for c in range(TT):
                more = c + 1 < TT
                scores(c)
                tokens(c)
                if c:
                    y_T(c - 1)
                for li in range(6):
                    products(c, li, 0)
                    products(c, li, 1)
                    fill(c, 0, li, 1)
                    merge(c, li, 0)
                    merge(c, li, 1)
                    if more and li == 0:
                        lora(c + 1)
                    if more and li == 1:
                        key_norm(c + 1)
                fill(c, 0, 6, 2)
                solve(c)
                fill(c, 1, 2, 3)
                if more:
                    state(c)
                fill(c, 1, 5, 3)
                outputs(c)

            for j in range(4):
                if j == 1:
                    y_T(TT - 1)
                u = U_VB + j
                q = u % NSPL
                take(u)
                for kk_ in range(2):
                    k = 2 * j + kk_
                    w = slice(512 * kk_, 512 * kk_ + 512)
                    for t in range(TT):
                        ts = slice(t * P, (t + 1) * P)
                        ins = three(PS[:, VB_BANK[t], :], hT_hi[:, k, ts], hT_lo[:, k, ts], w_hi[:, q, w], w_lo[:, q, w],
                                    k == 0, k == KD - 1)
                ins.then_inc(w_used, 1)

            def attn_scores(k):
                h, t = k // TT, k % TT
                r = slice(HD * (h % 2), HD * (h % 2) + HD)
                if t == 0 and h % 2 == 0:
                    pe.wait_ge(qk_loaded[h // 2], 16)
                if k >= 2:
                    pe.wait_ge(sc_ready, k - 1)
                else:
                    pe.wait_ge(vb_ready, TT)
                    pe.wait_ge(bonv_ready, TT)
                    pe.wait_ge(gate_ready, TT)
                pe.matmul(PS[:, 2 + k % 2, 0:P * (t + 1)], qkT[r, h - h % 2, t * P:(t + 1) * P],
                          qkT[r, h - h % 2 + 1, 0:P * (t + 1)], start=True, stop=True).then_inc(s_done, 1)

            def probs_T(k):
                t = k % TT
                pe.wait_ge(Pr_ready, k + 1)
                if k >= 2:
                    pe.wait_ge(PT_ready, k - 1)
                for j in range(t + 1):
                    ins = pe.transpose(PS[:, 4 + k % 2, j * P:(j + 1) * P], Pr[:, k % 2, j * P:(j + 1) * P], ident[:])
                ins.then_inc(pT_mm, 1)

            def values(k):
                h, t = k // TT, k % TT
                pe.wait_ge(PT_ready, k + 1)
                if t == 0 and h:
                    pe.wait_ge(O_ready, h)
                for j in range(t + 1):
                    ins = pe.matmul(PS[:, 6, t * HD:(t + 1) * HD], PT[:, k % 2, j, :],
                                    V_b[:, j, h * HD:(h + 1) * HD], start=j == 0, stop=j == t)
                ins.then_inc(pv_mm, 1)

            def out_T(p):
                pe.wait_ge(O_ready, 2 * p + 2)
                if p:
                    pe.wait_ge(obf_ready, p)
                for t in range(TT):
                    ins = pe.transpose(PS[:, 7, t * P:(t + 1) * P], O_sb[:, t, :], ident[:])
                ins.then_inc(oT_mm, 1)

            NK = TT * NH
            attn_scores(0)
            for k in range(NK):
                if k + 1 < NK:
                    attn_scores(k + 1)
                probs_T(k)
                if k:
                    values(k - 1)
                if k % 8 == 2 and k > 8:
                    out_T(k // 8 - 1)
            values(NK - 1)
            out_T(NP_ - 1)

            pe.wait_ge(oblo_ready, NP_)
            pe.wait_ge(yalo_ready, TT)
            with pe.Fori(0, 2) as i:
                for m in range(4):
                    u = U_GU + 12 * i + 3 * m
                    f = U_GU + 3 * m
                    b = 4 * (m % 2)
                    k = 4 * i + m
                    for g in range(2):
                        take(u + g)
                        if g == 0:
                            pe.wait_ge(gmul_ready, k + 1)
                        project(u + g, f + g, b + g).then_inc(w_used, 1)
                    take(u + 2)
                    project(u + 2, f + 2, b + 2, act_=(yaT_hi, yaT_lo), nk=4)
                    ins = project(u + 2, f + 2, b + 3, act_=(obT_hi, obT_lo), k0=4, nk=4)
                    ins.then_inc(w_used, 1)

            def by_rows(u, fourth, k, start, stop):
                q = fourth % NSPL
                take(u)
                for t in range(TT):
                    ts = slice(t * P, (t + 1) * P)
                    for h in range(2):
                        w = slice(512 * h, 512 * h + 512)
                        ins = three(PS[:, 2 * t + h, :], mixT_hi[:, k, ts], mixT_lo[:, k, ts], w_hi[:, q, w],
                                    w_lo[:, q, w], start, stop)
                ins.then_inc(w_used, 1)

            pe.wait_ge(mixlo_ready, KD)
            for k in range(KD):
                by_rows(U_WO + k, U_WO + k, k, k == 0, k == KD - 1)
            pe.wait_ge(x2_ready, TT)
            transposes(1, xn2)

            with pe.Fori(0, FT // 2) as i:
                for j in range(2):
                    k = 2 * i + j
                    for g in range(2):
                        u = U_FI + 4 * i + 2 * j + g
                        f = U_FI + 2 * j + g
                        take(u)
                        if g == 0:
                            pe.wait_ge(prod_ready, k + 1)
                        project(u, f, 2 * j + g, fresh=KD if j == g == 0 else None).then_inc(w_used, 1)

            def down(u, fourth, k, start, stop):
                q = fourth % NSPL
                take(u)
                for m in range(KD):
                    w = slice(m * P, (m + 1) * P)
                    rows = (act_hi[:, k, :], act_lo[:, k, :]) if isinstance(k, int) else \
                        tuple(a[:, bass.ds(k, 1), :].rearrange("p a b -> p (a b)") for a in (act_hi, act_lo))
                    ins = three(PS[:, m, :], w_hi[:, q, w], w_lo[:, q, w], rows[0], rows[1], start, stop)
                ins.then_inc(w_used, 1)

            pe.wait_ge(actlo_ready, FT)
            down(U_FO, U_FO, 0, True, False)
            with pe.Fori(0, (FT - 2) // 4) as i:
                for j in range(4):
                    down(U_FO + 1 + 4 * i + j, U_FO + 1 + j, 4 * i + 1 + j, False, False)
            down(U_FO + FT - 1, U_FO + FT - 1, FT - 1, False, True)
            pe.wait_ge(zT_ready, KD)
            for t in range(TT):
                for m in range(KD):
                    ins = pe.transpose(PS[:, 2 * t + m // 4, (m % 4) * P:(m % 4 + 1) * P],
                                       zT[:, m, t * P:(t + 1) * P], ident[:])
                ins.then_inc(z_T, 1)


_INS = ["x", "norm_mix_g", "w_in", "mu_shift", "w0", "w_decay_up", "a0", "w_iclr_up", "w_gate_up", "k_k", "k_a",
        "r_k", "ln_x_w", "ln_x_b", "w_up_a", "w_up_b", "w_o", "norm_ffn_g", "w_ffn_in", "w_ffn_out", "norm_final_g"]


def kernel(**inputs):
    import numpy as _np
    import concourse.bacc as _bacc
    from concourse import mybir as _mybir
    from concourse.bass_utils import run_bass_kernel_spmd as _run

    nc = _bacc.Bacc("TRN2", target_bir_lowering=False, num_devices=1)
    arrays, args = {}, []
    for name in _INS:
        a = _np.ascontiguousarray(inputs[name])
        arrays[f"in_{name}_dram"] = a
        args.append(nc.dram_tensor(f"in_{name}_dram", a.shape, _mybir.dt.from_np(a.dtype), kind="ExternalInput").ap())
    args.append(nc.dram_tensor("out_0_dram", (1, T, D), _mybir.dt.float32, kind="ExternalOutput").ap())
    build(nc, *args)
    r = _run(nc, [arrays], core_ids=[0])
    return r.results[0]["out_0_dram"]
```

```python
from contextlib import ExitStack

import concourse.bass as bass
from concourse import mybir

F32 = mybir.dt.float32
F32R = mybir.dt.float32r
U32 = mybir.dt.uint32
ALU = mybir.AluOpType
ACT = mybir.ActivationFunctionType
AX = mybir.AxisListType

P = 128
D = 1024
T = 512
KD = D // P
TT = T // P
HD = 64
AW = 512
NP_ = AW // P
NH = AW // HD
GL = 160
GH = GL // 2
F = 2816
FT = F // P
RMS_EPS = 1e-6
GN_EPS = 64e-5
CDEC = 0.6065306597126334
BIG = 1e30
LEVELS = [2, 4, 8, 16, 32, 64]

C_R, C_K, C_V = 0, 512, 1024
C_WD, C_GD = 1536, 1664
C_Q = 1824
C_KB, C_VB = C_Q + 512, C_Q + 1024
C_GA = C_Q + 1536
C_GB = C_GA + D

U_LORA = 0
U_RKV = 3
U_QK = 15
U_VB = 23
U_GATE = 27
U_UP = 43
U_WO = 51
U_FI = 59
U_FO = 103
N_UNITS = U_FO + FT
N_SHIFT = 15
WO_ORDER = [2, 3, 0, 1]
Z_ORDER = [4, 5, 6, 7, 0, 1, 2, 3]
RKV_TILE = [4, 5, 6, 7, 0, 1, 2, 3, 8, 9, 10, 11]
VB_BANK = [0, 5, 6, 7]
NRAW = 4
NSPL = 2

PC = {}
_at = 0
for _n, _k in (("mu", 12), ("mu_wa", 1), ("mu_g", 2), ("w0", 4), ("a0", 4), ("k_k", 4), ("k_a", 4),
               ("r_k", 4), ("ln_w", 4), ("ln_b", 4), ("g_mix", 8), ("g_ffn", 8)):
    PC[_n] = (_at, _k)
    _at += _k
NPAR = _at


def build(nc, x, norm_mix_g, w_in, mu_shift, w0, w_decay_up, a0, w_iclr_up, w_gate_up, k_k, k_a, r_k,
          ln_x_w, ln_x_b, w_up_a, w_up_b, w_o, norm_ffn_g, w_ffn_in, w_ffn_out, norm_final_g, out):
    xd = x[0].rearrange("(t p) d -> p t d", p=P)
    outd = out[0].rearrange("(t p) d -> p t d", p=P)
    w_in, w_up_a, w_up_b, w_o = w_in[0], w_up_a[0], w_up_b[0], w_o[0]
    w_ffn_in, w_ffn_out = w_ffn_in[0], w_ffn_out[0]

    with ExitStack() as ctx:
        at = [(nc.sbuf_base + 31) // 32 * 32]

        def sb(name, shape, dt=F32):
            t = nc.alloc_sbuf_tensor_at(name, shape, dt, offset=at[0])
            n = 4
            for s in shape[1:]:
                n *= s
            at[0] += (n + 31) // 32 * 32
            assert at[0] <= nc.sbuf_usable_end, (name, at[0])
            return t

        def sem(name):
            return ctx.enter_context(nc.semaphore(name))

        PS = ctx.enter_context(nc.psum_tensor("PS", [P, 8, 512], F32))

        ident = sb("ident", [P, P])
        blk1 = sb("blk1", [P, P])
        par = sb("par", [P, NPAR])
        qk_dram = nc.dram_tensor("qk_scratch", (2 * NP_, P, T), F32).ap()
        omka = sb("omka", [P, 4])
        hT_hi = sb("hT_hi", [P, KD, T], F32R)
        hT_lo = sb("hT_lo", [P, KD, T], F32R)
        wraw = sb("wraw", [P, NRAW, 1024])
        w_hi = sb("w_hi", [P, NSPL, 1024], F32R)
        w_lo = sb("w_lo", [P, NSPL, 1024], F32R)
        ss = sb("ss", [P, 3, TT])
        rstd = sb("rstd", [P, 3, TT])
        warm = sb("warm", [P, 4])
        base = at[0]

        yaT_hi = sb("yaT_hi", [P, NP_, T], F32R)
        yaT_lo = sb("yaT_lo", [P, NP_, T], F32R)
        mixers = at[0]
        at[0] = base
        raw = sb("raw", [P, 2, 516])
        rawd = sb("rawd", [P, 2, 512])
        lmix = sb("lmix", [P, 3, 512])
        assert at[0] <= mixers
        at[0] = base
        stage = sb("stage", [P, 2, NP_, T])
        at[0] = mixers

        xt = sb("xt", [P, TT, D])
        xn = sb("xn", [P, TT, D])
        junk = sb("junk", [P, D])
        prow = sb("prow", [P, P])
        tmpi = sb("tmpi", [P, P])

        at[0] = mixers
        rkvT = sb("rkvT", [P, 12, T])
        wupda = sb("wupda", [P, AW])
        wupg = sb("wupg", [GH, 2, AW])
        loraT = sb("loraT", [P, T])
        gdT = sb("gdT", [GH, 2, T])
        m_st = sb("m_st", [P, P])
        m_si = sb("m_si", [P, 2, P])
        lmask = sb("lmask", [P, 6, P])
        umask = sb("umask", [P, HD])
        resets = sb("resets", [P, 4 * P])
        kkE_R = sb("kkE_R", [P, 2, NP_, 2, P])
        Bt = sb("Bt", [P, NP_, P])
        Kt = sb("Kt", [P, NP_, P])
        V_tok = sb("V_tok", [P, AW])
        B_tok = sb("B_tok", [P, AW])
        K_tok = sb("K_tok", [P, AW])
        M_ts = sb("M_ts", [P, NH, P])
        MT_rb = sb("MT_rb", [P, NH, 2, P])
        LK_rk = sb("LK_rk", [P, NH, 2, P])
        Tm = sb("Tm", [P, NH, P])
        TmT = sb("TmT", [P, NH, P])
        PR = sb("PR", [P, 2, 4, P])
        G_sb = PR[:, 0].rearrange("p h (two d) -> p (h two) d", two=2)
        U_sb = sb("U_sb", [P, NH, HD])
        S_sb = sb("S_sb", [P, NP_, HD])
        S_tmp = sb("S_tmp", [P, NP_, HD])
        sg = sb("sg", [P, NP_, P])
        X = sb("X", [P, NP_, P])
        x63 = sb("x63", [P, NP_])
        gmid = sb("gmid", [P, NP_])
        gend = sb("gend", [P, NP_])
        gg = sb("gg", [P, NP_])
        Ep = sb("Ep", [P, NP_, P])
        Ee = sb("Ee", [P, NP_, P])
        En = sb("En", [P, NP_, P])
        aT = sb("aT", [P, NP_, P])
        kk = sb("kk", [P, NP_, P])
        sq = sb("sq", [P, NP_, P])
        rinv = sq
        kp = sb("kp", [P, NP_, P])
        rk = sb("rk", [P, NP_, P])
        bonv = sb("bonv", [P, NP_, P])
        gsb = sb("gsb", [P, NP_, P])
        ysum = sb("ysum", [P, NH])
        yvar = sb("yvar", [P, NH])
        yc = sb("yc", [P, NH, HD])
        yT = sb("yT", [P, NP_, P])
        ysq = yT[:].rearrange("p a (b d) -> p (a b) d", d=HD)

        at[0] = mixers
        obT_hi = sb("obT_hi", [P, NP_, T], F32R)
        obT_lo = sb("obT_lo", [P, NP_, T], F32R)
        mixed = at[0]
        V_b = sb("V_b", [P, TT, AW])
        qkT = sb("qkT", [P, 2 * NP_, T])
        dist = sb("dist", [P, T])
        alibi = sb("alibi", [P, 2, T])
        sc = sb("sc", [P, 2, T])
        Pr = sb("Pr", [P, 2, T])
        PT = sb("PT", [P, 2, TT, P])
        nmax = sb("nmax", [P, 2, TT])
        rsum = sb("rsum", [P, 2, TT])
        rrec = sb("rrec", [P, 2, TT])
        O_sb = sb("O_sb", [P, TT, P])
        obf = sb("obf", [P, T])

        at[0] = mixed
        mixT_hi = sb("mixT_hi", [P, KD, T], F32R)
        mixT_lo = sb("mixT_lo", [P, KD, T], F32R)
        gmul = sb("gmul", [P, 2, 2, T])
        msum = sb("msum", [P, 2, T])

        at[0] = base
        act_hi = sb("act_hi", [P, FT, T], F32R)
        act_lo = sb("act_lo", [P, FT, T], F32R)
        x2 = sb("x2", [P, TT, D])
        at_gates = at[0]
        sgf = sb("sgf", [P, 2, T])
        gact = sb("gact", [P, 2, T])
        prod = sb("prod", [P, 2, T])
        at[0] = at_gates
        gates = sb("gates", [P, KD, 2, T])
        gfin = sb("gfin", [P, D])
        at[0] = base
        xn2 = sb("xn2", [P, TT, D])
        junk2 = sb("junk2", [P, D])
        at[0] = base
        zT = sb("zT", [P, KD, T])
        x3 = sb("x3", [P, TT, D])
        fin = sb("fin", [P, TT, D])
        junk3 = sb("junk3", [P, D])

        w_loaded = [sem(f"w_loaded{i}") for i in range(NRAW)]
        w_hi_ready = sem("w_hi_ready")
        w_lo_ready = sem("w_lo_ready")
        w_used = sem("w_used")
        prow_zero = sem("prow_zero")
        warm_set = sem("warm_set")
        par_loaded_pool = sem("par_loaded_pool")
        par_loaded_sp = sem("par_loaded_sp")
        x_loaded = [sem(f"x_loaded{i}") for i in range(TT)]
        lora_w_loaded = sem("lora_w_loaded")
        consts = sem("consts")
        par_T = sem("par_T")
        par_ready = sem("par_ready")
        omka_ready = sem("omka_ready")
        ss_ready = sem("ss_ready")
        ms_ready = sem("ms_ready")
        std_ready = sem("std_ready")
        rstd_ready = sem("rstd_ready")
        xn_ready = sem("xn_ready")
        xT_ready = sem("xT_ready")
        hhi_ready = sem("hhi_ready")
        hlo_ready = sem("hlo_ready")
        raw_ready = sem("raw_ready")
        rawd_ready = sem("rawd_ready")
        mixed_ready = sem("mixed_ready")
        lora_ready = sem("lora_ready")
        zeros_ready = sem("zeros_ready")
        pool_order = sem("pool_order")
        dve_order = sem("dve_order")
        kkf_sq = sem("kkf_sq")
        nrm2_mm = sem("nrm2_mm")
        nrm2_ready = sem("nrm2_ready")
        nrm_ready = sem("nrm_ready")
        rinv_ready = sem("rinv_ready")
        z_mm = sem("z_mm")
        za_mm = sem("za_mm")
        sg_ready = sem("sg_ready")
        a_ready = sem("a_ready")
        X_ready = sem("X_ready")
        gmid_ready = sem("gmid_ready")
        P_ready = sem("P_ready")
        E_ready = sem("E_ready")
        B_K_ready = sem("B_K_ready")
        kkE_R_ready = sem("kkE_R_ready")
        rk_ready = sem("rk_ready")
        gg_ready = sem("gg_ready")
        score_mm = sem("score_mm")
        score_ready = sem("score_ready")
        tok_mm = sem("tok_mm")
        tok_ready = sem("tok_ready")
        T_ident = sem("T_ident")
        T_first = sem("T_first")
        pr_mm = sem("pr_mm")
        pr_ready = sem("pr_ready")
        zz_mm = sem("zz_mm")
        T_ready = sem("T_ready")
        g_mm = sem("g_mm")
        G_ready = sem("G_ready")
        u_mm = sem("u_mm")
        U_ready = sem("U_ready")
        s_mm = sem("s_mm")
        S_ready = sem("S_ready")
        bonus_mm = sem("bonus_mm")
        bonv_ready = sem("bonv_ready")
        gate_mm = sem("gate_mm")
        gate_ready = sem("gate_ready")
        y_mm = sem("y_mm")
        yc_ready = sem("yc_ready")
        ysq_ready = sem("ysq_ready")
        yvar_ready = sem("yvar_ready")
        ystd_ready = sem("ystd_ready")
        yrstd_ready = sem("yrstd_ready")
        yn_ready = sem("yn_ready")
        yT_mm = sem("yT_mm")
        yT_ready = sem("yT_ready")
        ya_ready = sem("ya_ready")
        yahi_ready = sem("yahi_ready")
        yalo_ready = sem("yalo_ready")
        vb_ready = sem("vb_ready")
        fill_ready = sem("fill_ready")
        qk_stored = [sem(f"qk_stored{i}") for i in range(2)]
        qk_loaded = [sem(f"qk_loaded{i}") for i in range(NP_)]
        alibi_ready = sem("alibi_ready")
        s_done = sem("s_done")
        sc_ready = sem("sc_ready")
        Pr_ready = sem("Pr_ready")
        pT_mm = sem("pT_mm")
        PT_ready = sem("PT_ready")
        pv_mm = sem("pv_mm")
        rrec_ready = sem("rrec_ready")
        O_ready = sem("O_ready")
        oT_mm = sem("oT_mm")
        obhi_ready = sem("obhi_ready")
        obf_ready = sem("obf_ready")
        oblo_ready = sem("oblo_ready")
        gates_stored = sem("gates_stored")
        sgate_ready = sem("sgate_ready")
        gmul_ready = sem("gmul_ready")
        msum_ready = sem("msum_ready")
        mixhi_ready = sem("mixhi_ready")
        mixlo_ready = sem("mixlo_ready")
        wo_mm = sem("wo_mm")
        z_mm_out = sem("z_mm_out")
        x_again = sem("x_again")
        x2_ready = sem("x2_ready")
        sgf_ready = sem("sgf_ready")
        gact_ready = sem("gact_ready")
        prod_ready = sem("prod_ready")
        acthi_ready = sem("acthi_ready")
        actlo_ready = sem("actlo_ready")
        zT_ready = sem("zT_ready")
        z_T = sem("z_T")
        x3_ready = sem("x3_ready")
        gfin_loaded = sem("gfin_loaded")
        fin_ready = sem("fin_ready")
        out_done = sem("out_done")

        def pc(name, i=0, n=None):
            o, k = PC[name]
            return par[:, o + i:o + i + (k if n is None else n)]

        def wide(col, n=P):
            return col.unsqueeze(2).to_broadcast([P, col.shape[1], n])

        def first(t, b):
            return t.rearrange("p h (q two r) -> p h q two r", two=2, r=b)[:, :, :, 0, :]

        def second(t, b):
            return t.rearrange("p h (q two r) -> p h q two r", two=2, r=b)[:, :, :, 1, :]

        def unit_width(u):
            return KD * GH if isinstance(u, int) and u in (U_LORA + 1, U_LORA + 2) else 1024

        def shift_bank(u):
            return 4 + u % 2 if u else 0

        def cols(bank, shape, **k):
            return PS[:, bank, :].rearrange(shape, **k)

        param_rows = ((mu_shift[0, 0:1536], "mu", P), (mu_shift[0, C_WD:C_WD + P], "mu_wa", P),
                      (mu_shift[0, C_GD:C_GD + GL], "mu_g", GH), (w0[0], "w0", P), (a0[0], "a0", P),
                      (k_k[0], "k_k", P), (k_a[0], "k_a", P), (r_k[0].rearrange("h d -> (h d)"), "r_k", P),
                      (ln_x_w[0], "ln_w", P), (ln_x_b[0], "ln_b", P), (norm_mix_g[0], "g_mix", P),
                      (norm_ffn_g[0], "g_ffn", P))

        def load_param(queue, row, loaded):
            src, name, wdt = row
            o, k = PC[name]
            queue.dma_start(prow[o:o + k, 0:wdt], src.rearrange("(r c) -> r c", c=wdt)).then_inc(loaded, 16)

        block = ctx.enter_context(nc.Block())

        @block.sync
        def _(sp):
            def start_unit(u, fourth):
                slot = fourth % NRAW
                if not isinstance(u, int) or u >= NRAW:
                    sp.wait_ge(w_lo_ready, u - NRAW + 1)
                return slot

            def load_cols(u, fourth, w, c0, n=P, k0=0):
                slot = start_unit(u, fourth)
                dst = wraw[:, slot, 0:8 * n].rearrange("p (k c) -> p k c", k=8)
                src = w.rearrange("(k p) c -> p k c", p=P)
                for h in range(2):
                    sp.dma_start(dst[:, 4 * h:4 * h + 4, :], src[:, 4 * h:4 * h + 4, bass.ds(c0, n)])\
                      .then_inc(w_loaded[slot], 16)

            def load_rows(u, fourth, w, r0):
                slot = start_unit(u, fourth)
                for h in range(2):
                    sp.dma_start(wraw[:, slot, 512 * h:512 * h + 512],
                                 w[bass.ds(r0, P), 512 * h:512 * h + 512]).then_inc(w_loaded[slot], 16)

            for t in range(TT):
                sp.dma_start(xt[:, t, :], xd[:, t, :]).then_inc(x_loaded[t], 16)
            sp.wait_ge(prow_zero, 1)
            for r in param_rows[1::2]:
                load_param(sp, r, par_loaded_sp)
            load_cols(U_LORA, U_LORA, w_in, C_WD)
            for h in range(2):
                load_cols(U_LORA + 1 + h, U_LORA + 1 + h, w_in, C_GD + GH * h, n=GH)
            load_cols(U_RKV, U_RKV, w_in, RKV_TILE[0] * P)
            sp.wait_ge(xT_ready, KD)
            sp.dma_start(wupda[0:HD, :], w_decay_up[0]).then_inc(lora_w_loaded, 16)
            sp.dma_start(wupda[HD:P, :], w_iclr_up[0]).then_inc(lora_w_loaded, 16)
            sp.dma_start(wupg[:], w_gate_up[0].rearrange("(h p) c -> p h c", p=GH)).then_inc(lora_w_loaded, 16)
            for j in range(1, 12):
                load_cols(U_RKV + j, U_RKV + j, w_in, RKV_TILE[j] * P)
            def store_qk(n):
                sp.wait_ge(fill_ready, n + 1)
                sp.dma_start(qk_dram[n].rearrange("p (a b) -> p a b", a=NP_), stage[:, n % 2, :, T - P:T])\
                  .then_inc(qk_stored[n % 2], 16)

            for n in range(2 * NP_):
                u = U_QK + n
                load_cols(u, u, w_in, (C_KB if n % 2 else C_Q) + P * (n // 2))
                if n >= 4:
                    store_qk(n - 4)
            for j in range(4):
                u = U_VB + j
                slot = start_unit(u, u)
                for h in range(2):
                    sp.dma_start(wraw[:, slot, 512 * h:512 * h + 512],
                                 w_in[(2 * j + h) * P:(2 * j + h + 1) * P, C_VB:C_VB + AW])\
                      .then_inc(w_loaded[slot], 16)
                store_qk(4 + j)
            def load_gates(k, fourth):
                load_cols(U_GATE + 2 * k, fourth, w_in, C_GA + k * P)
                load_cols(U_GATE + 2 * k + 1, fourth + 1, w_in, C_GB + k * P)

            load_gates(0, U_GATE)
            sp.wait_ge(y_mm, TT)
            for i in range(2):
                sp.wait_ge(qk_stored[i], 16 * NP_)
            for p in range(NP_):
                sp.dma_start(qkT[:, 2 * p:2 * p + 2, :], qk_dram[2 * p:2 * p + 2].rearrange("n p t -> p n t"))\
                  .then_inc(qk_loaded[p], 16)
            load_gates(1, U_GATE + 2)
            with sp.Fori(1, KD // 2) as i:
                for m in range(2):
                    load_gates(2 * i + m, U_GATE + 2 * m)
            sp.wait_ge(yalo_ready, TT)
            for t in range(TT):
                sp.dma_start(x2[:, t, :], xd[:, t, :]).then_inc(x_again, 16)
            with sp.Fori(0, KD // 4) as i:
                for m in range(4):
                    slot = start_unit(U_UP + 4 * i + m, U_UP + m)
                    dst = wraw[:, slot, :].rearrange("p (k c) -> p k c", k=8)
                    for h, w in enumerate((w_up_a, w_up_b)):
                        sp.dma_start(dst[:, 4 * h:4 * h + 4, :],
                                     w.rearrange("(k p) c -> p k c", p=P)[:, :, bass.ds((4 * i + m) * P, P)])\
                          .then_inc(w_loaded[slot], 16)
            for k in range(KD):
                load_rows(U_WO + k, U_WO + k, w_o, P * k)
            with sp.Fori(0, FT // 2) as i:
                for j in range(2):
                    u = U_FI + 4 * i + 2 * j
                    f = U_FI + 2 * j
                    load_cols(u, f, w_ffn_in, (2 * i + j) * P)
                    load_cols(u + 1, f + 1, w_ffn_in, F + (2 * i + j) * P)
            load_rows(U_FO, U_FO, w_ffn_out, 0)
            with sp.Fori(0, (FT - 2) // 4) as i:
                for j in range(4):
                    load_rows(U_FO + 1 + 4 * i + j, U_FO + 1 + j, w_ffn_out, (4 * i + 1 + j) * P)
            load_rows(U_FO + FT - 1, U_FO + FT - 1, w_ffn_out, (FT - 1) * P)
            sp.wait_ge(actlo_ready, FT)
            sp.dma_start(gfin[:], norm_final_g.partition_broadcast(P)).then_inc(gfin_loaded, 16)
            for t in range(TT):
                sp.wait_ge(fin_ready, t + 1)
                sp.dma_start(outd[:, t, :], fin[:, t, :]).then_inc(out_done, 16)
            sp.wait_ge(out_done, 16 * TT)

        @block.gpsimd
        def _(pool):
            n = [0]

            def link(ins):
                n[0] += 1
                ins.then_inc(pool_order, 1)
                pool.wait_ge(pool_order, n[0])

            pool.memset(warm[:], 1.0).then_inc(warm_set, 1)
            pool.memset(prow[:], 0.0).then_inc(prow_zero, 1)
            pool.wait_ge(prow_zero, 1)
            for r in param_rows[0::2]:
                load_param(pool, r, par_loaded_pool)

            link(pool.memset(tmpi[:], 1.0))
            link(pool.affine_select(out=ident[:], in_=tmpi[:], compare_op=ALU.is_equal, fill=0.0, base=0,
                                    pattern=[[-1, P]], channel_multiplier=1))
            link(pool.memset(blk1[:], 0.0))
            pool.memset(blk1[0:HD, 0:HD], 1.0)
            link(pool.memset(blk1[HD:P, HD:P], 1.0))
            pool.memset(ss[:, 2, :], 0.0).then_inc(consts, 1)
            pool.memset(raw[:, :, 0:1], 0.0).then_inc(zeros_ready, 1)
            pool.wait_ge(xT_ready, KD)
            pool.wait_ge(par_ready, 1)
            link(pool.memset(m_st[:], 1.0))
            link(pool.affine_select(out=m_st[:], in_=m_st[:], compare_op=ALU.is_ge, fill=0.0, base=-1,
                                    pattern=[[-1, P]], channel_multiplier=1))
            link(pool.memset(m_si[:], 1.0))
            for i in range(2):
                link(pool.affine_select(out=m_si[:, i, :], in_=m_si[:, i, :], compare_op=ALU.is_ge, fill=0.0,
                                        base=i - 1, pattern=[[1, P]], channel_multiplier=-1))
            link(pool.memset(resets[:], 1.0))
            link(pool.memset(resets[:].rearrange("p (a b) -> p a b", b=P)[:, :, 0:1], 0.0))
            link(pool.memset(lmask[:], -1.0))
            for li, b in enumerate([1] + LEVELS[:-1]):
                v = lmask[:, li, :].rearrange("p (q two r) -> p q two r", two=2, r=b)
                nq = HD // b
                f = v[:, :, 0, :]
                link(pool.affine_select(out=f, in_=f, compare_op=ALU.is_ge, fill=0.0, base=-b,
                                        pattern=[[-2 * b, nq], [0, b]], channel_multiplier=1))
                link(pool.affine_select(out=f, in_=f, compare_op=ALU.is_ge, fill=0.0, base=2 * b - 1,
                                        pattern=[[2 * b, nq], [0, b]], channel_multiplier=-1))
                link(pool.memset(v[:, :, 1, :], 0.0))
                link(pool.affine_select(out=lmask[:, li, :], in_=lmask[:, li, :], compare_op=ALU.not_equal, fill=1.0,
                                        base=0, pattern=[[-1, P]], channel_multiplier=1))
            link(pool.memset(umask[:], 0.0))
            for fill, above in ((-1.0, 0), (1.0, 1)):
                link(pool.affine_select(out=umask[:], in_=umask[:], compare_op=ALU.not_equal, fill=fill,
                                        base=-above, pattern=[[-2, HD]], channel_multiplier=1))
            for h in range(NH):
                pool.tensor_copy(M_ts[:, h, :], ident[:])
                pool.tensor_copy(MT_rb[:, h, 0, :], ident[:])
            pool.memset(MT_rb[:, :, 1, :], 0.0)
            pool.memset(LK_rk[:], 0.0).then_inc(zeros_ready, 1)

            def keys(c):
                kc = rkvT[:, 4:8, c * P:(c + 1) * P]
                if c:
                    pool.wait_ge(nrm2_mm, c)
                else:
                    pool.wait_ge(mixed_ready, U_RKV + 4)
                link(pool.tensor_tensor(kk[:], kc, wide(pc("k_k")), ALU.mult))
                pool.tensor_tensor(sq[:], kk[:], kk[:], ALU.mult).then_inc(kkf_sq, 1)

            def factors(c):
                par_ = c % 2
                cs = slice(c * P, (c + 1) * P)
                r_c, k_c = rkvT[:, 0:4, cs], rkvT[:, 4:8, cs]
                pool.wait_ge(a_ready, c + 1)
                link(pool.tensor_tensor(kp[:], aT[:], wide(pc("k_a")), ALU.mult))
                link(pool.tensor_tensor(kp[:], kp[:], wide(omka[:]), ALU.add))
                link(pool.tensor_tensor(kp[:], kp[:], k_c, ALU.mult))
                pool.wait_ge(X_ready, c + 1)
                link(pool.tensor_tensor(X[:], X[:], wide(x63[:]), ALU.subtract))
                pool.tensor_tensor(sg[:], X[:], sg[:], ALU.subtract).then_inc(P_ready, 1)
                pool.wait_ge(rinv_ready, c + 1)
                link(pool.tensor_tensor(kk[:], kk[:], rinv[:], ALU.mult))
                if c:
                    pool.wait_ge(tok_mm, 3 * c)
                    pool.wait_ge(score_mm, 10 * c)
                link(pool.tensor_tensor(Bt[:], kk[:], aT[:], ALU.mult))
                pool.wait_ge(E_ready, c + 1)
                pool.tensor_tensor(Bt[:], Bt[:], En[:], ALU.mult)
                pool.tensor_tensor(Kt[:], kp[:], En[:], ALU.mult).then_inc(B_K_ready, 1)
                if c >= 2:
                    pool.wait_ge(y_mm, c - 1)
                if c == 0:
                    pool.wait_ge(mixed_ready, U_RKV + 8)
                pool.tensor_tensor(kkE_R[:, par_, :, 0, :], kk[:], Ee[:], ALU.mult)
                pool.tensor_tensor(kkE_R[:, par_, :, 1, :], r_c, Ep[:], ALU.mult).then_inc(kkE_R_ready, 1)
                if c:
                    pool.wait_ge(bonus_mm, c)
                    if c > 1:
                        pool.wait_ge(S_ready, c - 1)
                    pool.wait_ge(gmid_ready, c + 1)
                    link(pool.tensor_tensor(gg[:], gend[:], gmid[:], ALU.mult))
                    pool.tensor_copy(gend[:], Ep[:, :, P - 1]).then_inc(gg_ready, 1)
                else:
                    pool.tensor_copy(gend[:], Ep[:, :, P - 1])
                link(pool.tensor_tensor(rk[:], r_c, kp[:], ALU.mult))
                pool.tensor_tensor(rk[:], rk[:], wide(pc("r_k")), ALU.mult).then_inc(rk_ready, 1)

            def inverse_start(c):
                if c:
                    pool.wait_ge(u_mm, 2 * c)
                for h in range(NH):
                    pool.tensor_copy(second(Tm[:, h:h + 1, :], 1)[:, 0], ident[:].rearrange("p (q two) -> p q two", two=2)[:, :, 1:2])
                    ins = pool.tensor_copy(first(TmT[:, h:h + 1, :], 1)[:, 0], ident[:].rearrange("p (q two) -> p q two", two=2)[:, :, 0:1])
                ins.then_inc(T_ident, 1)

            def after_y(c):
                pool.wait_ge(yc_ready, c + 1)
                if c:
                    pool.wait_ge(yalo_ready, c)
                pool.tensor_tensor(ysq, yc[:], yc[:], ALU.mult).then_inc(ysq_ready, 1)

            def after_y2(c):
                pool.wait_ge(yrstd_ready, c + 1)
                pool.tensor_tensor(yT[:].rearrange("p i (two d) -> p two i d", two=2),
                                   yc[:].rearrange("p (two i) d -> p two i d", two=2),
                                   wide(yvar[:], HD).rearrange("p (two i) d -> p two i d", two=2),
                                   ALU.mult).then_inc(yn_ready, 1)

            def after_y3(c):
                pool.wait_ge(yT_ready, c + 1)
                pool.wait_ge(bonv_ready, c + 1)
                link(pool.tensor_tensor(yT[:], yT[:], bonv[:], ALU.add))
                pool.wait_ge(gate_ready, c + 1)
                pool.tensor_tensor(yT[:], yT[:], gsb[:], ALU.mult).then_inc(ya_ready, 1)

            keys(0)
            factors(0)
            inverse_start(0)
            for c in range(TT):
                if c + 1 < TT:
                    keys(c + 1)
                if c:
                    after_y3(c - 1)
                if c + 1 < TT:
                    factors(c + 1)
                after_y(c)
                if c + 1 < TT:
                    inverse_start(c + 1)
                after_y2(c)
            after_y3(TT - 1)

            pool.wait_ge(yahi_ready, TT)
            pool.wait_ge(yalo_ready, TT)
            link(pool.iota(dist[:].bitcast(mybir.dt.int32), pattern=[[-1, T]], base=T - P, channel_multiplier=1))
            link(pool.tensor_copy(sc[:, 0, :], dist[:].bitcast(mybir.dt.int32)))
            link(pool.affine_select(out=dist[:], in_=sc[:, 0, :], compare_op=ALU.is_ge, fill=BIG, base=T - P,
                                    pattern=[[-1, T]], channel_multiplier=1))
            pool.tensor_scalar(alibi[:, 0, :], dist[:], 0.5, None, ALU.mult).then_inc(alibi_ready, 1)
            pool.tensor_scalar(alibi[:, 1, :], dist[:], 0.25, None, ALU.mult).then_inc(alibi_ready, 1)
            for h in range(2, NH):
                pool.wait_ge(sc_ready, TT * (h - 1))
                pool.tensor_scalar(alibi[:, h % 2, :], alibi[:, h % 2, :], 0.25, None, ALU.mult)\
                    .then_inc(alibi_ready, 1)

            with pool.Fori(0, KD // 2) as i:
                for j in range(2):
                    pool.wait_ge(gmul_ready, 2 * i + j + 3)
                    pool.tensor_tensor(msum[:, j, :], gmul[:, j, 0, :], gmul[:, j, 1, :], ALU.add)\
                        .then_inc(msum_ready, 1)

        @block.scalar
        def _(act):
            def split_hi(u, fourth):
                s = fourth % NRAW
                act.wait_ge(w_loaded[s], (u - fourth % NRAW) // NRAW * 32 + 32 if isinstance(u, int)
                            else (u - s) * (32 // NRAW) + 32)
                if not isinstance(u, int) or u >= NSPL:
                    act.wait_ge(w_used, u - NSPL + 1)
                n = unit_width(u)
                act.activation(w_hi[:, fourth % NSPL, 0:n], wraw[:, s, 0:n], ACT.Copy).then_inc(w_hi_ready, 1)

            def squares(src, junk_, which, t, ready, tile=None):
                tile = t if tile is None else tile
                act.wait_ge(*ready)
                if which or t:
                    act.wait_ge(ss_ready, which * TT + t)
                act.activation(junk_[:], src[:, tile, :], ACT.Square, accum_out=ss[:, which, t:t + 1])\
                   .then_inc(ss_ready, 1)

            def std(k):
                act.wait_ge(ms_ready, k + 1)
                act.activation(rstd[:, k // TT, k % TT:k % TT + 1], ss[:, k // TT, k % TT:k % TT + 1], ACT.Sqrt)\
                   .then_inc(std_ready, 1)

            act.wait_ge(warm_set, 1)
            act.activation(warm[:, 1:2], warm[:, 0:1], ACT.Sqrt)
            for t in range(TT):
                squares(xt, junk, 0, t, (x_loaded[t], 16))
                if t:
                    std(t - 1)
            std(TT - 1)
            split_hi(0, 0)
            split_hi(1, 1)

            def h_hi(which, name):
                for k in range(KD):
                    act.wait_ge(xT_ready, which * KD + k + 1)
                    if which == 0 and k == 0:
                        act.wait_ge(par_ready, 1)
                    act.activation(hT_hi[:, k, :], PS[:, k, :], ACT.Copy, scale=pc(name, k, 1))\
                       .then_inc(hhi_ready, 1)

            h_hi(0, "g_mix")

            def raw_tile(u):
                act.wait_ge(w_used, u + 1)
                if u >= 2:
                    act.wait_ge(mixed_ready, u - 1)
                act.activation(raw[:, u % 2, 1:T + 1], PS[:, shift_bank(u), :], ACT.Copy).then_inc(raw_ready, 1)

            def lora_inputs():
                act.wait_ge(mixed_ready, U_LORA + 3)
                act.activation(loraT[0:HD, :], lmix[0:HD, 0, :], ACT.Tanh)
                act.activation(loraT[HD:P, :], lmix[HD:P, 0, :], ACT.Copy).then_inc(lora_ready, 1)
                act.activation(gdT[:], lmix[0:GH, 1:3, :], ACT.Sigmoid).then_inc(lora_ready, 1)

            def sigmoids(c):
                act.wait_ge(z_mm, c + 1)
                for p in range(NP_):
                    ins = act.activation(sg[:, p, :], cols(2, "p (a b) -> p a b", b=P)[:, p, :], ACT.Sigmoid,
                                         bias=pc("w0", p, 1))
                ins.then_inc(sg_ready, 1)
                act.wait_ge(za_mm, c + 1)
                if c:
                    act.wait_ge(B_K_ready, c)
                for p in range(NP_):
                    ins = act.activation(aT[:, p, :], cols(3, "p (a b) -> p a b", b=P)[:, p, :], ACT.Sigmoid,
                                         bias=pc("a0", p, 1))
                ins.then_inc(a_ready, 1)

            def exps(c):
                act.wait_ge(X_ready, c + 1)
                if c > 1:
                    act.wait_ge(gg_ready, c - 1)
                act.activation(gmid[:], x63[:], ACT.Exp, scale=-CDEC).then_inc(gmid_ready, 1)
                act.wait_ge(P_ready, c + 1)
                if c:
                    act.wait_ge(kkE_R_ready, c)
                    act.wait_ge(rk_ready, c)
                act.activation(Ep[:], X[:], ACT.Exp, scale=-CDEC)
                act.activation(En[:], X[:], ACT.Exp, scale=CDEC)
                act.activation(Ee[:], sg[:], ACT.Exp, scale=-CDEC).then_inc(E_ready, 1)

            def norms(c):
                act.wait_ge(nrm2_ready, c + 1)
                act.activation(rinv[:], rinv[:], ACT.Sqrt).then_inc(nrm_ready, 1)

            def tokens(c):
                for i, (dst, bank) in enumerate(((V_tok, 2), (B_tok, 3), (K_tok, 0))):
                    act.wait_ge(tok_mm, 3 * c + i + 1)
                    if c and i == 0:
                        act.wait_ge(s_mm, c)
                        act.wait_ge(y_mm, c)
                    act.activation(dst[:], PS[:, bank, :], ACT.Copy).then_inc(tok_ready, 1)

            def merge(c, li, half):
                b = LEVELS[li]
                k = 12 * c + 2 * li + half
                hs = slice(4 * half, 4 * half + 4)
                z = cols(6 + half, "p (k h q r) -> p k h q r", k=2, h=4, r=b)
                act.wait_ge(zz_mm, k + 1)
                if li == 4:
                    lo, hi = slice(HD * half, HD * half + 32), slice(HD * half + 32, HD * half + HD)
                    act.activation(Tm[hi, :, lo], PS[hi, 6 + half, 0:256].rearrange("p (h c) -> p h c", c=32),
                                   ACT.Copy)
                    act.activation(TmT[lo, :, hi], PS[lo, 6 + half, 256:512].rearrange("p (h c) -> p h c", c=32),
                                   ACT.Copy).then_inc(T_ready, 1)
                elif li < 5:
                    act.activation(first(Tm[:, hs, :], b), z[:, 0], ACT.Copy)
                    act.activation(second(TmT[:, hs, :], b), z[:, 1], ACT.Copy).then_inc(T_ready, 1)
                else:
                    act.activation(TmT[0:HD, hs, HD:P], PS[0:HD, 6 + half, 0:256].rearrange("p (h d) -> p h d", d=HD),
                                   ACT.Copy).then_inc(T_ready, 1)

            def minus_u(c):
                for half in range(2):
                    act.wait_ge(u_mm, 2 * c + half + 1)
                    if c:
                        act.wait_ge(s_mm, c)
                        act.wait_ge(y_mm, c)
                    act.activation(U_sb[:, 4 * half:4 * half + 4, :],
                                   PS[:, 6 + half, 0:256].rearrange("p (h d) -> p h d", d=HD), ACT.Copy,
                                   scale=-1.0).then_inc(U_ready, 1)

            def gate_out(c):
                act.wait_ge(gate_mm, c + 1)
                if c:
                    act.wait_ge(ya_ready, c)
                act.activation(gsb[:].rearrange("p a b -> p (a b)"), PS[:, 3, :], ACT.Copy).then_inc(gate_ready, 1)

            def ystd(c):
                act.wait_ge(yvar_ready, c + 1)
                act.activation(yvar[:], yvar[:], ACT.Sqrt).then_inc(ystd_ready, 1)

            def y_affine(c):
                act.wait_ge(yT_mm, c + 1)
                if c:
                    act.wait_ge(yalo_ready, c)
                for p in range(NP_):
                    ins = act.activation(yT[:, p, :], cols(1, "p (a b) -> p a b", b=P)[:, p, :], ACT.Identity,
                                         bias=pc("ln_b", p, 1), scale=pc("ln_w", p, 1))
                ins.then_inc(yT_ready, 1)

            def ya_hi(c):
                act.wait_ge(ya_ready, c + 1)
                if c == TT - 1:
                    for i in range(2):
                        act.wait_ge(qk_stored[i], 16 * NP_)
                act.activation(yaT_hi[:, :, c * P:(c + 1) * P], yT[:], ACT.Copy).then_inc(yahi_ready, 1)

            for u in range(N_SHIFT):
                split_hi(u + 2, u + 2)
                raw_tile(u)
                if u == 3:
                    lora_inputs()
                if u == 5:
                    sigmoids(0)
                if u == 9:
                    norms(0)
                if u == 11:
                    exps(0)
            def fill_out(n):
                act.wait_ge(w_used, U_QK + n + 1)
                if n >= 2:
                    act.wait_ge(qk_stored[n % 2], 16 * (n // 2))
                act.activation(stage[:, n % 2, :, T - P:T], cols(1 if n % 2 else 7, "p (a b) -> p a b", b=P), ACT.Copy,
                               scale=1.0 if n % 2 else -HD ** -0.5).then_inc(fill_ready, 1)

            for c in range(TT):
                more = c + 1 < TT
                fill_out(2 * c)
                tokens(c)
                if c:
                    y_affine(c - 1)
                merge(c, 0, 0)
                merge(c, 0, 1)
                if more:
                    sigmoids(c + 1)
                merge(c, 1, 0)
                merge(c, 1, 1)
                if more:
                    norms(c + 1)
                merge(c, 2, 0)
                merge(c, 2, 1)
                if c:
                    ya_hi(c - 1)
                merge(c, 3, 0)
                merge(c, 3, 1)
                if more:
                    exps(c + 1)
                for li in range(4, 6):
                    merge(c, li, 0)
                    merge(c, li, 1)
                split_hi(U_QK + 2 * c + 2, U_QK + 2 * c + 2)
                gate_out(c)
                minus_u(c)
                fill_out(2 * c + 1)
                split_hi(U_QK + 2 * c + 3, U_QK + 2 * c + 3)
                ystd(c)
            split_hi(U_VB + 2, U_VB + 2)
            y_affine(TT - 1)
            split_hi(U_VB + 3, U_VB + 3)
            ya_hi(TT - 1)
            for j in range(2, 4):
                split_hi(U_VB + j + 2, U_VB + j + 2)

            act.wait_ge(yalo_ready, TT)
            act.wait_ge(w_used, U_VB + 4)
            for t in range(TT):
                act.activation(V_b[:, t, :], PS[:, VB_BANK[t], :], ACT.Copy).then_inc(vb_ready, 1)

            def probs(h, t):
                k = TT * h + t
                n = P * (t + 1)
                act.wait_ge(sc_ready, k + 1)
                if k >= 2:
                    act.wait_ge(pT_mm, k - 1)
                act.activation(Pr[:, k % 2, 0:n], sc[:, k % 2, 0:n], ACT.Exp, bias=nmax[:, h % 2, t:t + 1],
                               scale=-1.0, accum_out=rsum[:, h % 2, t:t + 1]).then_inc(Pr_ready, 1)

            def probs_T(k):
                n = P * (k % TT + 1)
                act.wait_ge(pT_mm, k + 1)
                if k >= 2:
                    act.wait_ge(pv_mm, k - 1)
                act.activation(PT[:, k % 2].rearrange("p a b -> p (a b)")[:, 0:n], PS[:, 4 + k % 2, 0:n], ACT.Copy)\
                   .then_inc(PT_ready, 1)

            def ob_hi(p):
                act.wait_ge(obf_ready, p + 1)
                act.activation(obT_hi[:, p, :], obf[:], ACT.Copy).then_inc(obhi_ready, 1)

            for p in range(NP_):
                for k in range(8 * p, 8 * p + 8):
                    probs(k // TT, k % TT)
                    if k >= 1:
                        probs_T(k - 1)
                    if k % 2:
                        split_hi(U_GATE + k // 2 + 2, U_GATE + k // 2 + 2)
                    if k % 8 == 3 and p:
                        ob_hi(p - 1)
            probs_T(8 * NP_ - 1)
            ob_hi(NP_ - 1)

            act.wait_ge(gates_stored, 2 * KD)

            def mix_hi(k):
                act.wait_ge(msum_ready, k + 1)
                act.activation(mixT_hi[:, k, :], msum[:, k % 2, :], ACT.Copy).then_inc(mixhi_ready, 1)

            for k in range(KD):
                if k == 1:
                    act.wait_ge(oblo_ready, NP_)
                act.activation(gates[:, k], gates[:, k], ACT.Sigmoid).then_inc(sgate_ready, 1)
                split_hi(U_UP + k + 2, U_UP + k + 2)
                if k:
                    mix_hi(k - 1)
            mix_hi(KD - 1)

            for k in range(KD - 1):
                split_hi(U_WO + k + 2, U_WO + k + 2)
            act.activation(warm[:, 2:3], warm[:, 0:1], ACT.Sqrt)
            for n, t in enumerate(WO_ORDER):
                squares(x2, junk2, 1, n, (x2_ready, n + 1), t)
                std(TT + n)
            split_hi(U_FI + 1, U_FI + 1)
            h_hi(1, "g_ffn")

            with act.Fori(0, FT // 2) as i:
                for j in range(2):
                    u = U_FI + 4 * i + 2 * j
                    f = U_FI + 2 * j
                    split_hi(u + 2, f + 2)
                    act.wait_ge(w_used, u + 1)
                    act.activation(sgf[:, j, :], PS[:, 2 * j, :], ACT.Sigmoid).then_inc(sgf_ready, 1)
                    split_hi(u + 3, f + 3)
                    act.wait_ge(prod_ready, 2 * i + j + 3)
                    act.activation(act_hi[:, bass.ds(2 * i + j, 1), :], prod[:, j:j + 1, :], ACT.Copy)\
                       .then_inc(acthi_ready, 1)

            with act.Fori(0, (FT - 2) // 4) as i:
                for j in range(4):
                    split_hi(U_FO + 2 + 4 * i + j, U_FO + 2 + j)
            for n in range(1, KD, 2):
                m = Z_ORDER[n]
                act.wait_ge(z_mm_out, n + 1)
                act.activation(zT[:, m, :], PS[:, m, :], ACT.Copy).then_inc(zT_ready, 1)
            act.activation(warm[:, 3:4], warm[:, 0:1], ACT.Sqrt)
            for t in range(TT):
                squares(x3, junk3, 2, t, (x3_ready, t + 1))
                std(2 * TT + t)

        @block.vector
        def _(dve):
            n = [0]

            def link(ins):
                n[0] += 1
                ins.then_inc(dve_order, 1)
                dve.wait_ge(dve_order, n[0])

            def split_lo(u, fourth):
                s, q = fourth % NRAW, fourth % NSPL
                dve.wait_ge(w_hi_ready, u + 1)
                n = unit_width(u)
                dve.tensor_tensor(w_lo[:, q, 0:n], wraw[:, s, 0:n], w_hi[:, q, 0:n].bitcast(F32), ALU.subtract)\
                   .then_inc(w_lo_ready, 1)

            def mean_square(which, t):
                k = which * TT + t
                dve.wait_ge(ss_ready, k + 1)
                s = ss[:, which, t:t + 1]
                dve.tensor_scalar(s, s, 1.0 / D, RMS_EPS, ALU.mult, ALU.add).then_inc(ms_ready, 1)

            def norm(src, dst, which, t, tile=None):
                tile = t if tile is None else tile
                k = which * TT + t
                dve.wait_ge(std_ready, k + 1)
                r = rstd[:, which, t:t + 1]
                dve.reciprocal(r, r).then_inc(rstd_ready, 1)
                dve.wait_ge(rstd_ready, k + 1)
                if dst is not None:
                    dve.tensor_scalar(dst[:, tile, :], src[:, tile, :], r, None, ALU.mult).then_inc(xn_ready, 1)

            def h_lo(which, name):
                for k in range(KD):
                    dve.wait_ge(hhi_ready, which * KD + k + 1)
                    dve.scalar_tensor_tensor(out=hT_lo[:, k, :], in0=PS[:, k, :], scalar=pc(name, k, 1),
                                             in1=hT_hi[:, k, :].bitcast(F32), op0=ALU.mult, op1=ALU.subtract)\
                       .then_inc(hlo_ready, 1)

            for t in range(TT):
                mean_square(0, t)
                if t:
                    norm(xt, xn, 0, t - 1)
            norm(xt, xn, 0, TT - 1)
            dve.wait_ge(par_T, 1)
            dve.tensor_copy(par[:], PS[:, 7, T - P:T - P + NPAR]).then_inc(par_ready, 1)
            dve.wait_ge(par_ready, 1)
            dve.tensor_scalar(omka[:], pc("k_a"), -1.0, 1.0, ALU.mult, ALU.add).then_inc(omka_ready, 1)
            split_lo(0, 0)
            split_lo(1, 1)
            h_lo(0, "g_mix")

            def shift(u):
                np_, j = P, u % 2
                if u == U_LORA:
                    dst, mu = lmix[:, 0, :], pc("mu_wa")
                elif u < U_RKV:
                    np_ = GH
                    dst, mu = lmix[0:GH, u, :], par[0:GH, PC["mu_g"][0] + u - 1:PC["mu_g"][0] + u]
                else:
                    tile = RKV_TILE[u - U_RKV]
                    dst, mu = rkvT[:, tile, :], pc("mu", tile, 1)
                dve.wait_ge(raw_ready, u + 1)
                dve.tensor_tensor(rawd[0:np_, j, :], raw[0:np_, j, 0:T], raw[0:np_, j, 1:T + 1], ALU.subtract)\
                   .then_inc(rawd_ready, 1)
                dve.wait_ge(rawd_ready, u + 1)
                dve.scalar_tensor_tensor(out=dst, in0=rawd[0:np_, j, :], scalar=mu, in1=raw[0:np_, j, 1:T + 1],
                                         op0=ALU.mult, op1=ALU.add).then_inc(mixed_ready, 1)

            def key_norm(c):
                dve.wait_ge(nrm2_mm, c + 1)
                dve.tensor_scalar(rinv[:], cols(0, "p (a b) -> p a b", b=P), 1e-24, None, ALU.max)\
                   .then_inc(nrm2_ready, 1)

            def key_norm2(c):
                dve.wait_ge(nrm_ready, c + 1)
                dve.reciprocal(rinv[:], rinv[:]).then_inc(rinv_ready, 1)

            def decay_sums(c):
                dve.wait_ge(sg_ready, c + 1)
                if c:
                    dve.wait_ge(E_ready, c)
                link(dve.tensor_tensor_scan(X[:].rearrange("p a b -> p (a b)"), resets[:],
                                            sg[:].rearrange("p a b -> p (a b)"), 0.0, ALU.mult, ALU.add))
                if c:
                    dve.wait_ge(gmid_ready, c)
                dve.tensor_copy(x63[:], X[:, :, HD - 1]).then_inc(X_ready, 1)

            def scores(c):
                for q in range(10):
                    dve.wait_ge(score_mm, 10 * c + q + 1)
                    if c and q == 0:
                        dve.wait_ge(y_mm, c)
                    odd = q % 2
                    if q < 2:
                        dst = M_ts[:, 4 * odd:4 * odd + 4, :]
                        mask = m_st[:].unsqueeze(1).to_broadcast([P, 4, P])
                        src = cols(q % 4, "p (h t) -> p h t", h=4)
                    else:
                        h = 4 * odd + 2 * ((q - 2) % 4 // 2)
                        dst = (MT_rb if q < 6 else LK_rk)[:, h:h + 2]
                        mask = m_si[:].unsqueeze(1).to_broadcast([P, 2, 2, P])
                        src = cols(q % 4, "p (h k t) -> p h k t", h=2, k=2)
                    dve.copy_predicated(out=dst, mask=mask.bitcast(U32), data=src).then_inc(score_ready, 1)

            def first_merge(c):
                dve.wait_ge(T_ident, c + 1)
                dve.wait_ge(score_ready, 10 * c + 6)
                for half in range(2):
                    hs = slice(4 * half, 4 * half + 4)
                    dve.tensor_tensor(first(Tm[:, hs, :], 1), first(M_ts[:, hs, :], 1),
                                      lmask[:, 0, 0:P:2].unsqueeze(1).unsqueeze(3).to_broadcast([P, 4, HD, 1]),
                                      ALU.mult)
                    dve.tensor_tensor(second(TmT[:, hs, :], 1), second(MT_rb[:, hs, 0, :], 1),
                                      umask[:].unsqueeze(1).unsqueeze(3).to_broadcast([P, 4, HD, 1]), ALU.mult)\
                       .then_inc(T_first, 1)

            def merge(c, li, half):
                k = 12 * c + 2 * li + half
                dve.wait_ge(pr_mm, k + 1)
                w = cols(4 + half, "p (h c) -> p h c", h=4)
                if li == 4:
                    r = slice(HD * half + 32, HD * half + HD)
                    dve.tensor_scalar(PR[r].rearrange("p a h c -> p (a h) c")[:, :, 0:32],
                                      PS[r, 4 + half, 0:256].rearrange("p (h c) -> p h c", c=32), -1.0, None,
                                      ALU.mult).then_inc(pr_ready, 1)
                elif li < 5:
                    dve.tensor_tensor(PR[:, half], w, lmask[:, li + 1, :].unsqueeze(1).to_broadcast([P, 4, P]),
                                      ALU.mult).then_inc(pr_ready, 1)
                else:
                    dve.tensor_scalar(PR[HD:P, half, :, 0:HD], w[HD:P, :, 0:HD], -1.0, None, ALU.mult)\
                       .then_inc(pr_ready, 1)

            def state_g(c):
                for half in range(2):
                    dve.wait_ge(g_mm, 2 * c + half + 1)
                    dve.tensor_copy(G_sb[:, 4 * half:4 * half + 4, :],
                                    PS[:, 4 + half, 0:256].rearrange("p (h d) -> p h d", d=HD)).then_inc(G_ready, 1)

            def bonus(c):
                dve.wait_ge(bonus_mm, c + 1)
                if c:
                    dve.wait_ge(ya_ready, c)
                dve.tensor_tensor(bonv[:], cols(2, "p (a b) -> p a b", b=P), rkvT[:, 8:12, c * P:(c + 1) * P],
                                  ALU.mult).then_inc(bonv_ready, 1)

            def state(c):
                src = PS[:, 0, 0:256].rearrange("p (a d) -> p a d", d=HD)
                dve.wait_ge(s_mm, c + 1)
                dve.wait_ge(gg_ready, c + 1)
                if c:
                    link(dve.tensor_tensor(S_tmp[:], src, S_sb[:], ALU.add))
                    dve.wait_ge(y_mm, c + 1)
                    dve.tensor_tensor(S_sb[:], S_tmp[:], wide(gg[:], HD), ALU.mult).then_inc(S_ready, 1)
                else:
                    dve.tensor_tensor(S_sb[:], src, wide(gg[:], HD), ALU.mult).then_inc(S_ready, 1)

            def y_centre(c):
                y = PS[:, 1:5:3, 0:256]
                dve.wait_ge(y_mm, c + 1)
                link(dve.tensor_reduce(ysum[:].rearrange("p (a b) -> p a b", a=2),
                                       y.rearrange("p a (b d) -> p a b d", d=HD), AX.X, ALU.add))
                if c:
                    dve.wait_ge(yT_mm, c)
                dve.scalar_tensor_tensor(out=yc[:].rearrange("p (a b) d -> p a b d", a=2),
                                         in0=wide(ysum[:], HD).rearrange("p (a b) d -> p a b d", a=2),
                                         scalar=-1.0 / HD, in1=y.rearrange("p a (b d) -> p a b d", d=HD),
                                         op0=ALU.mult, op1=ALU.add).then_inc(yc_ready, 1)

            def y_var(c):
                dve.wait_ge(ysq_ready, c + 1)
                link(dve.tensor_reduce(yvar[:], ysq, AX.X, ALU.add))
                dve.tensor_scalar(yvar[:], yvar[:], 1.0 / HD, GN_EPS, ALU.mult, ALU.add).then_inc(yvar_ready, 1)

            def y_rstd(c):
                dve.wait_ge(ystd_ready, c + 1)
                dve.reciprocal(yvar[:], yvar[:]).then_inc(yrstd_ready, 1)

            def ya_lo(c):
                cs = slice(c * P, (c + 1) * P)
                dve.wait_ge(yahi_ready, c + 1)
                dve.tensor_tensor(yaT_lo[:, :, cs], yT[:], yaT_hi[:, :, cs].bitcast(F32), ALU.subtract)\
                   .then_inc(yalo_ready, 1)

            dve.wait_ge(zeros_ready, 1)
            for u in range(N_SHIFT):
                split_lo(u + 2, u + 2)
                shift(u)
                if u == 6:
                    dve.wait_ge(zeros_ready, 2)
                    decay_sums(0)
                if u == 9:
                    key_norm(0)
                if u == 10:
                    key_norm2(0)
            for c in range(TT):
                more = c + 1 < TT
                scores(c)
                first_merge(c)
                merge(c, 0, 0)
                merge(c, 0, 1)
                if c:
                    split_lo(U_QK + 2 * c + 1, U_QK + 2 * c + 1)
                merge(c, 1, 0)
                merge(c, 1, 1)
                if more:
                    key_norm(c + 1)
                    decay_sums(c + 1)
                merge(c, 2, 0)
                merge(c, 2, 1)
                if more:
                    key_norm2(c + 1)
                merge(c, 3, 0)
                merge(c, 3, 1)
                if c:
                    ya_lo(c - 1)
                for li in range(4, 6):
                    merge(c, li, 0)
                    merge(c, li, 1)
                split_lo(U_QK + 2 * c + 2, U_QK + 2 * c + 2)
                state_g(c)
                bonus(c)
                if more:
                    state(c)
                else:
                    split_lo(U_VB + 1, U_VB + 1)
                y_centre(c)
                y_var(c)
                y_rstd(c)
            split_lo(U_VB + 2, U_VB + 2)
            split_lo(U_VB + 3, U_VB + 3)
            ya_lo(TT - 1)

            for j in range(2, 4):
                split_lo(U_VB + j + 2, U_VB + j + 2)

            dve.memset(ss[:, 0, 0:1], 0.0).then_inc(gmul_ready, 2)

            def score_bias(h, t):
                k = TT * h + t
                w = P * (t + 1)
                dve.wait_ge(s_done, k + 1)
                dve.wait_ge(alibi_ready, h + 1)
                if k >= 2:
                    dve.wait_ge(Pr_ready, k - 1)
                dve.tensor_tensor_reduce(sc[:, k % 2, 0:w], PS[:, 2 + k % 2, 0:w], alibi[:, h % 2, T - w:T],
                                         1.0, 3e38, ALU.add, ALU.min, nmax[:, h % 2, t:t + 1]).then_inc(sc_ready, 1)

            def attn_out(h):
                dve.wait_ge(Pr_ready, TT * (h + 1))
                dve.reciprocal(rrec[:, h % 2, :], rsum[:, h % 2, :]).then_inc(rrec_ready, 1)
                dve.wait_ge(rrec_ready, h + 1)
                dve.wait_ge(pv_mm, TT * (h + 1))
                if h >= 2 and h % 2 == 0:
                    dve.wait_ge(oT_mm, h // 2)
                dve.tensor_tensor(O_sb[:, :, HD * (h % 2):HD * (h % 2) + HD],
                                  PS[:, 6, 0:256].rearrange("p (t d) -> p t d", d=HD), wide(rrec[:, h % 2, :], HD),
                                  ALU.mult).then_inc(O_ready, 1)

            def ob_lo(p):
                dve.wait_ge(obhi_ready, p + 1)
                dve.tensor_tensor(obT_lo[:, p, :], obf[:], obT_hi[:, p, :].bitcast(F32), ALU.subtract)\
                   .then_inc(oblo_ready, 1)

            def ob_copy(p):
                dve.wait_ge(oT_mm, p + 1)
                dve.tensor_copy(obf[:], PS[:, 7, :]).then_inc(obf_ready, 1)

            for h in range(NH):
                p = h // 2
                for t in range(TT):
                    score_bias(h, t)
                    if t == 1 and h:
                        attn_out(h - 1)
                    if t % 2:
                        n_gate = (TT * h + t) // 2
                        split_lo(U_GATE + n_gate + 2, U_GATE + n_gate + 2)
                        dve.wait_ge(w_used, U_GATE + n_gate + 1)
                        dve.tensor_copy(gates[:, n_gate // 2, n_gate % 2, :], PS[:, n_gate % 2, :])\
                           .then_inc(gates_stored, 1)
                    if t == 3 and h % 2 == 0 and p:
                        ob_copy(p - 1)
                if h % 2 == 1 and p:
                    ob_lo(p - 1)
            attn_out(NH - 1)
            ob_copy(NP_ - 1)
            ob_lo(NP_ - 1)

            def mix_lo(k):
                dve.wait_ge(mixhi_ready, k + 1)
                dve.tensor_tensor(mixT_lo[:, k, :], msum[:, k % 2, :], mixT_hi[:, k, :].bitcast(F32), ALU.subtract)\
                   .then_inc(mixlo_ready, 1)

            for k in range(KD):
                split_lo(U_UP + k + 2, U_UP + k + 2)
                dve.wait_ge(sgate_ready, k + 1)
                dve.wait_ge(w_used, U_UP + k + 1)
                dve.tensor_tensor(gmul[:, k % 2], gates[:, k], PS[:, 2 * (k % 2):2 * (k % 2) + 2, :], ALU.mult)\
                   .then_inc(gmul_ready, 1)
                if k:
                    mix_lo(k - 1)
            mix_lo(KD - 1)

            for k in range(KD - 1):
                split_lo(U_WO + k + 2, U_WO + k + 2)
            dve.memset(ss[:, 0, 0:1], 0.0).then_inc(prod_ready, 2)
            dve.wait_ge(x_again, 16 * TT)
            for n, t in enumerate(WO_ORDER):
                if n < TT - 1:
                    dve.wait_ge(wo_mm, n + 1)
                else:
                    dve.wait_ge(w_used, U_WO + KD)
                dve.tensor_tensor(x2[:, t, :].rearrange("p (a b) -> p a b", a=2),
                                  x2[:, t, :].rearrange("p (a b) -> p a b", a=2), PS[:, 2 * t:2 * t + 2, :],
                                  ALU.add).then_inc(x2_ready, 1)
                if n:
                    mean_square(1, n - 1)
                    norm(x2, xn2, 1, n - 1, WO_ORDER[n - 1])
            mean_square(1, TT - 1)
            norm(x2, xn2, 1, TT - 1, WO_ORDER[TT - 1])
            split_lo(U_FI + 1, U_FI + 1)
            h_lo(1, "g_ffn")

            with dve.Fori(0, FT // 2) as i:
                for j in range(2):
                    u = U_FI + 4 * i + 2 * j
                    f = U_FI + 2 * j
                    k = 2 * i + j
                    split_lo(u + 2, f + 2)
                    dve.wait_ge(sgf_ready, k + 1)
                    dve.tensor_tensor(gact[:, j, :], sgf[:, j, :], PS[:, 2 * j, :], ALU.mult).then_inc(gact_ready, 1)
                    split_lo(u + 3, f + 3)
                    dve.wait_ge(gact_ready, k + 1)
                    dve.wait_ge(w_used, u + 2)
                    dve.tensor_tensor(prod[:, j, :], gact[:, j, :], PS[:, 2 * j + 1, :], ALU.mult)\
                       .then_inc(prod_ready, 1)
                    dve.wait_ge(acthi_ready, k + 1)
                    dve.tensor_tensor(act_lo[:, bass.ds(k, 1), :], prod[:, j:j + 1, :],
                                      act_hi[:, bass.ds(k, 1), :].bitcast(F32), ALU.subtract)\
                       .then_inc(actlo_ready, 1)

            with dve.Fori(0, (FT - 2) // 4) as i:
                for j in range(4):
                    split_lo(U_FO + 2 + 4 * i + j, U_FO + 2 + j)
            for n in range(0, KD, 2):
                m = Z_ORDER[n]
                dve.wait_ge(z_mm_out, n + 1)
                dve.tensor_copy(zT[:, m, :], PS[:, m, :]).then_inc(zT_ready, 1)
            def finish(t):
                mean_square(2, t)
                norm(None, None, 2, t)
                if t == 0:
                    dve.wait_ge(gfin_loaded, 16)
                dve.scalar_tensor_tensor(out=fin[:, t, :], in0=x3[:, t, :], scalar=rstd[:, 2, t:t + 1],
                                         in1=gfin[:], op0=ALU.mult, op1=ALU.mult).then_inc(fin_ready, 1)

            for t in range(TT):
                dve.wait_ge(z_T, t + 1)
                dve.tensor_tensor(x3[:, t, :].rearrange("p (a b) -> p a b", a=2),
                                  x2[:, t, :].rearrange("p (a b) -> p a b", a=2), PS[:, 2 * t:2 * t + 2, :],
                                  ALU.add).then_inc(x3_ready, 1)
                if t:
                    finish(t - 1)
            finish(TT - 1)

        @block.tensor
        def _(pe):
            def three(out_, a_hi, a_lo, b_hi, b_lo, start, stop):
                pe.matmul(out_, a_hi, b_hi, start=start, stop=False)
                pe.matmul(out_, a_hi, b_lo, start=False, stop=False)
                return pe.matmul(out_, a_lo, b_hi, start=False, stop=stop)

            def project(u, fourth, bank, width=P, act_=(hT_hi, hT_lo), k0=0, nk=KD, fresh=None):
                q = fourth % NSPL
                for k in range(nk):
                    if fresh is not None:
                        pe.wait_ge(hlo_ready, fresh + k + 1)
                    w = slice((k0 + k) * width, (k0 + k + 1) * width)
                    ins = three(PS[0:width, bank, :], w_hi[:, q, w], w_lo[:, q, w], act_[0][:, k, :],
                                act_[1][:, k, :], k == 0, k == nk - 1)
                return ins

            def take(u):
                pe.wait_ge(w_lo_ready, u + 1)

            def transposes(which, src, order):
                for n, t in enumerate(order):
                    pe.wait_ge(xn_ready, which * TT + n + 1)
                    if which == 0 and n == TT - 1:
                        pe.wait_ge(par_loaded_pool, 16 * len(param_rows[0::2]))
                        pe.wait_ge(par_loaded_sp, 16 * len(param_rows[1::2]))
                        pe.transpose(PS[:, 7, T - P:T - P + NPAR], prow[0:NPAR, :], ident[0:NPAR, 0:NPAR])\
                          .then_inc(par_T, 1)
                        pe.wait_ge(par_ready, 1)
                    for k in range(KD):
                        ins = pe.transpose(PS[:, k, t * P:(t + 1) * P], src[:, t, k * P:(k + 1) * P], ident[:])
                        if n == TT - 1:
                            ins.then_inc(xT_ready, 1)

            pe.wait_ge(consts, 1)
            transposes(0, xn, range(TT))

            def lora(c):
                cs = slice(c * P, (c + 1) * P)
                if c:
                    pe.wait_ge(tok_ready, 3 * c)
                else:
                    pe.wait_ge(lora_ready, 2)
                    pe.wait_ge(lora_w_loaded, 48)
                for p in range(NP_):
                    ins = pe.matmul(PS[:, 2, p * P:(p + 1) * P], wupda[0:HD, p * P:(p + 1) * P], loraT[0:HD, cs],
                                    start=True, stop=True)
                ins.then_inc(z_mm, 1)
                for p in range(NP_):
                    ins = pe.matmul(PS[:, 3, p * P:(p + 1) * P], wupda[HD:P, p * P:(p + 1) * P], loraT[HD:P, cs],
                                    start=True, stop=True)
                ins.then_inc(za_mm, 1)

            def key_norm(c):
                pe.wait_ge(kkf_sq, c + 1)
                pe.matmul(PS[:, 0, :], blk1[:], sq[:].rearrange("p a b -> p (a b)"), start=True, stop=True)\
                  .then_inc(nrm2_mm, 1)

            def scores(c):
                par_ = c % 2
                def bank_free(q):
                    if q >= 4:
                        pe.wait_ge(score_ready, 10 * c + q - 3)
                    elif c:
                        pe.wait_ge(*((S_ready, c), (yc_ready, c), (bonv_ready, c), (gate_ready, c))[q])
                    else:
                        pe.wait_ge(*((nrm2_ready, 1), (hlo_ready, KD), (sg_ready, 1), (a_ready, 1))[q])

                fill(c, 0, 0, 3)
                pe.wait_ge(B_K_ready, c + 1)
                pe.wait_ge(kkE_R_ready, c + 1)
                for q in range(0, 10, 2):
                    bank_free(q)
                    bank_free(q + 1)
                    for i in range(4 if q < 2 else 2):
                        for odd in range(2):
                            r = slice(HD * odd, HD * odd + HD)
                            if q < 2:
                                ins = pe.matmul(PS[:, odd, i * P:(i + 1) * P], kkE_R[r, par_, i, 0, :],
                                                Bt[r, i, :], start=True, stop=True)
                            else:
                                p = 2 * ((q - 2) % 4 // 2) + i
                                ins = pe.matmul(PS[:, (q + odd) % 4, i * 2 * P:(i + 1) * 2 * P],
                                                (Bt if q < 6 else Kt)[r, p, :],
                                                kkE_R[r, par_, p, :, :].rearrange("p a b -> p (a b)"),
                                                start=True, stop=True)
                            if i == (3 if q < 2 else 1):
                                ins.then_inc(score_mm, 1)
                    fill(c, 0, 3 + q // 2, 1)

            def tokens(c):
                cs = slice(c * P, (c + 1) * P)
                for i, (bank, sd) in enumerate(((2, 7), (3, 8), (0, 9))):
                    pe.wait_ge(score_ready, 10 * c + sd)
                    for p in range(NP_):
                        src = (rkvT[:, 8 + p, cs], Bt[:, p, :], Kt[:, p, :])[i]
                        ins = pe.transpose(PS[:, bank, p * P:(p + 1) * P], src, ident[:])
                    ins.then_inc(tok_mm, 1)

            def products(c, li, half):
                k = 12 * c + 2 * li + half
                if li >= 4:
                    pe.wait_ge(T_ready, 12 * c + 2 * li)
                elif li:
                    pe.wait_ge(T_ready, k - 1)
                else:
                    pe.wait_ge(T_first, 2 * c + half + 1)
                    if c and half == 0:
                        pe.wait_ge(yc_ready, c)
                    if c:
                        pe.wait_ge(G_ready, 2 * (c - 1) + half + 1)
                if li == 4:
                    lo, hi = slice(HD * half, HD * half + 32), slice(HD * half + 32, HD * half + HD)
                    for h in range(NH):
                        ins = pe.matmul(PS[hi, 4 + half, 32 * h:32 * h + 32], MT_rb[lo, h, 0, hi], Tm[lo, h, lo],
                                        start=True, stop=True, tile_position=(HD * half, HD * half + 32))
                for i in range(4 if li != 4 else 0):
                    h = 4 * half + i
                    if li < 5:
                        ins = pe.matmul(PS[:, 4 + half, i * P:(i + 1) * P], MT_rb[:, h, 0, :], Tm[:, h, :],
                                        start=True, stop=True)
                    else:
                        ins = pe.matmul(PS[HD:P, 4 + half, i * P:i * P + HD], MT_rb[0:HD, h, 0, HD:P],
                                        Tm[0:HD, h, 0:HD], start=True, stop=True)
                ins.then_inc(pr_mm, 1)

            def merge(c, li, half):
                b = LEVELS[li]
                k = 12 * c + 2 * li + half
                pe.wait_ge(pr_ready, k + 1)
                if li == 0 and c:
                    pe.wait_ge(U_ready, 2 * (c - 1) + half + 1)
                if li == 0 and half:
                    pe.wait_ge(fill_ready, 2 * c + 1)
                if li == 4:
                    lo, hi = slice(HD * half, HD * half + 32), slice(HD * half + 32, HD * half + HD)
                    for h in range(NH):
                        w = PR[hi, h // 4, h % 4, 0:32]
                        pe.matmul(PS[hi, 6 + half, 32 * h:32 * h + 32], TmT[hi, h, hi], w, start=True, stop=True,
                                  tile_position=(HD * half + 32, HD * half + 32))
                        ins = pe.matmul(PS[lo, 6 + half, 256 + 32 * h:256 + 32 * h + 32], w, TmT[hi, h, hi],
                                        start=True, stop=True, tile_position=(HD * half + 32, HD * half))
                for i in range(4 if li != 4 else 0):
                    h = 4 * half + i
                    w = PR[:, half, i:i + 1, :]
                    if li < 5:
                        pe.matmul(PS[:, 6 + half, i * HD:(i + 1) * HD], TmT[:, h, :], first(w, b)[:, 0],
                                  start=True, stop=True)
                        ins = pe.matmul(PS[:, 6 + half, 256 + i * HD:256 + (i + 1) * HD], PR[:, half, i, :],
                                        second(TmT[:, h:h + 1, :], b)[:, 0], start=True, stop=True)
                    else:
                        ins = pe.matmul(PS[0:HD, 6 + half, i * HD:(i + 1) * HD], PR[HD:P, half, i, 0:HD],
                                        TmT[HD:P, h, HD:P], start=True, stop=True)
                ins.then_inc(zz_mm, 1)

            def fill(c, i, k0, nk):
                u = U_QK + 2 * c + i
                q = u % NSPL
                for k in range(k0, k0 + nk):
                    if k == 0:
                        take(u)
                        if i and c:
                            pe.wait_ge(yT_ready, c)
                    w = slice(k * P, (k + 1) * P)
                    ins = three(PS[:, 1 if i else 7, :], w_hi[:, q, w], w_lo[:, q, w], hT_hi[:, k, :], hT_lo[:, k, :], k == 0,
                                k == KD - 1)
                if k == KD - 1:
                    ins.then_inc(w_used, 1)

            def solve(c):
                par_ = c % 2
                pe.wait_ge(tok_ready, 3 * c + 3)
                pe.wait_ge(score_ready, 10 * c + 10)
                if c:
                    pe.wait_ge(S_ready, c)
                pe.wait_ge(pr_ready, 12 * (c + 1))
                for odd in range(2):
                    r = slice(HD * odd, HD * odd + HD)
                    for i in range(4):
                        h = 2 * i + odd
                        o = PS[:, 4 + odd, i * HD:(i + 1) * HD]
                        ins = pe.matmul(o, LK_rk[:, 4 * odd + i, 0, :], V_tok[:, h * HD:(h + 1) * HD], start=True,
                                        stop=c == 0)
                        if c:
                            ins = pe.matmul(o, kkE_R[r, par_, i, 0, :], S_sb[r, i, :], start=False, stop=True)
                    ins.then_inc(g_mm, 1)
                pe.wait_ge(rk_ready, c + 1)
                pe.wait_ge(sg_ready, min(c + 2, TT))
                pe.matmul(PS[:, 2, :], blk1[:], rk[:].rearrange("p a b -> p (a b)"), start=True, stop=True)\
                  .then_inc(bonus_mm, 1)
                pe.wait_ge(a_ready, min(c + 2, TT))
                for p in range(NP_):
                    for k in range(2):
                        ins = pe.matmul(PS[:, 3, p * P:(p + 1) * P], wupg[:, k, p * P:(p + 1) * P],
                                        gdT[:, k, c * P:(c + 1) * P], start=k == 0, stop=k == 1)
                ins.then_inc(gate_mm, 1)
                fill(c, 1, 4, 1)
                for half in range(2):
                    pe.wait_ge(G_ready, 2 * c + half + 1)
                    pe.wait_ge(T_ready, 12 * (c + 1))
                    for i in range(4):
                        h = 4 * half + i
                        ins = pe.matmul(PS[:, 6 + half, i * HD:(i + 1) * HD], TmT[:, h, :], G_sb[:, h, :],
                                        start=True, stop=True)
                    ins.then_inc(u_mm, 1)

            def state(c):
                pe.wait_ge(U_ready, 2 * c + 2)
                if c + 1 < TT:
                    pe.wait_ge(nrm2_ready, c + 2)
                for h in range(NH):
                    r = slice(HD * (h % 2), HD * (h % 2) + HD)
                    hc = slice(h * HD, (h + 1) * HD)
                    o = PS[r, 0, (h // 2) * HD:(h // 2 + 1) * HD]
                    pe.matmul(o, K_tok[:, hc], V_tok[:, hc], start=True, stop=False)
                    ins = pe.matmul(o, B_tok[:, hc], U_sb[:, 4 * (h % 2) + h // 2, :], start=False, stop=True)
                ins.then_inc(s_mm, 1)

            def outputs(c):
                par_ = c % 2
                pe.wait_ge(U_ready, 2 * c + 2)
                pe.wait_ge(G_ready, 2 * c + 1)
                for odd, bank in ((1, 4), (0, 1)):
                    if bank == 1:
                        pe.wait_ge(fill_ready, 2 * c + 2)
                    r = slice(HD * odd, HD * odd + HD)
                    for i in range(4):
                        h, sh = 2 * i + odd, 4 * odd + i
                        o = PS[:, bank, i * HD:(i + 1) * HD]
                        pe.matmul(o, LK_rk[:, sh, 1, :], V_tok[:, h * HD:(h + 1) * HD], start=True, stop=False)
                        ins = pe.matmul(o, MT_rb[:, sh, 1, :], U_sb[:, sh, :], start=False, stop=c == 0)
                        if c:
                            ins = pe.matmul(o, kkE_R[r, par_, i, 1, :], S_sb[r, i, :], start=False, stop=True)
                ins.then_inc(y_mm, 1)

            def y_T(c):
                pe.wait_ge(yn_ready, c + 1)
                if c + 1 < TT:
                    pe.wait_ge(score_ready, 10 * (c + 1) + 10)
                for p in range(NP_):
                    ins = pe.transpose(PS[:, 1, p * P:(p + 1) * P],
                                       yT[:, p, :], ident[:])
                ins.then_inc(yT_mm, 1)

            for u in range(N_SHIFT):
                take(u)
                if u >= 3:
                    pe.wait_ge(raw_ready, u - 1)
                project(u, u, shift_bank(u), GH if u in (U_LORA + 1, U_LORA + 2) else P, fresh=0 if u == 0 else None)\
                    .then_inc(w_used, 1)
                if u == 4:
                    lora(0)
                if u == 8:
                    key_norm(0)
            for c in range(TT):
                more = c + 1 < TT
                scores(c)
                if c == 0:
                    pe.wait_ge(raw_ready, N_SHIFT)
                    pe.wait_ge(mixed_ready, N_SHIFT)
                tokens(c)
                if c:
                    y_T(c - 1)
                for li in range(6):
                    products(c, li, 0)
                    if li >= 4:
                        fill(c, 1, 2 * li - 8, 1)
                    products(c, li, 1)
                    if li >= 4:
                        fill(c, 1, 2 * li - 7, 1)
                    merge(c, li, 0)
                    merge(c, li, 1)
                    if more and li == 0:
                        lora(c + 1)
                    if more and li == 1:
                        key_norm(c + 1)
                solve(c)
                fill(c, 1, 5, 2)
                if more:
                    state(c)
                fill(c, 1, 7, 1)
                outputs(c)

            for j in range(4):
                if j == 1:
                    y_T(TT - 1)
                u = U_VB + j
                q = u % NSPL
                take(u)
                for kk_ in range(2):
                    k = 2 * j + kk_
                    w = slice(512 * kk_, 512 * kk_ + 512)
                    for t in range(TT):
                        ts = slice(t * P, (t + 1) * P)
                        ins = three(PS[:, VB_BANK[t], :], hT_hi[:, k, ts], hT_lo[:, k, ts], w_hi[:, q, w], w_lo[:, q, w],
                                    k == 0, k == KD - 1)
                ins.then_inc(w_used, 1)

            def attn_scores(k):
                h, t = k // TT, k % TT
                r = slice(HD * (h % 2), HD * (h % 2) + HD)
                if t == 0 and h % 2 == 0:
                    pe.wait_ge(qk_loaded[h // 2], 16)
                if k >= 2:
                    pe.wait_ge(sc_ready, k - 1)
                else:
                    pe.wait_ge(vb_ready, TT)
                    pe.wait_ge(bonv_ready, TT)
                    pe.wait_ge(gate_ready, TT)
                pe.matmul(PS[:, 2 + k % 2, 0:P * (t + 1)], qkT[r, h - h % 2, t * P:(t + 1) * P],
                          qkT[r, h - h % 2 + 1, 0:P * (t + 1)], start=True, stop=True).then_inc(s_done, 1)

            def probs_T(k):
                t = k % TT
                pe.wait_ge(Pr_ready, k + 1)
                if k >= 2:
                    pe.wait_ge(PT_ready, k - 1)
                for j in range(t + 1):
                    ins = pe.transpose(PS[:, 4 + k % 2, j * P:(j + 1) * P], Pr[:, k % 2, j * P:(j + 1) * P], ident[:])
                ins.then_inc(pT_mm, 1)

            def values(k):
                h, t = k // TT, k % TT
                pe.wait_ge(PT_ready, k + 1)
                if t == 0 and h:
                    pe.wait_ge(O_ready, h)
                for j in range(t + 1):
                    ins = pe.matmul(PS[:, 6, t * HD:(t + 1) * HD], PT[:, k % 2, j, :],
                                    V_b[:, j, h * HD:(h + 1) * HD], start=j == 0, stop=j == t)
                ins.then_inc(pv_mm, 1)

            def out_T(p):
                pe.wait_ge(O_ready, 2 * p + 2)
                if p:
                    pe.wait_ge(obf_ready, p)
                for t in range(TT):
                    ins = pe.transpose(PS[:, 7, t * P:(t + 1) * P], O_sb[:, t, :], ident[:])
                ins.then_inc(oT_mm, 1)

            def gate(k):
                n = k // 2
                u = U_GATE + n
                q = u % NSPL
                if k % 2 == 0:
                    take(u)
                    if n >= 2:
                        pe.wait_ge(gates_stored, n - 1)
                    elif n:
                        pe.wait_ge(yT_ready, TT)
                    else:
                        pe.wait_ge(vb_ready, 1)
                for kt in range(4 * (k % 2), 4 * (k % 2) + 4):
                    w = slice(kt * P, (kt + 1) * P)
                    ins = three(PS[:, n % 2, :], w_hi[:, q, w], w_lo[:, q, w], hT_hi[:, kt, :], hT_lo[:, kt, :],
                                kt == 0, kt == KD - 1)
                if k % 2:
                    ins.then_inc(w_used, 1)

            NK = TT * NH
            gate(0)
            attn_scores(0)
            for k in range(NK):
                if k + 1 < NK:
                    attn_scores(k + 1)
                    gate(k + 1)
                probs_T(k)
                if k:
                    values(k - 1)
                if k % 8 == 2 and k > 8:
                    out_T(k // 8 - 1)
            values(NK - 1)
            out_T(NP_ - 1)

            pe.wait_ge(yalo_ready, TT)
            pe.wait_ge(gates_stored, 2 * KD)
            with pe.Fori(0, KD // 4) as i:
                for m in range(4):
                    u = U_UP + 4 * i + m
                    b = 2 * (m % 2)
                    take(u)
                    pe.wait_ge(gmul_ready, 4 * i + m + 1)
                    project(u, U_UP + m, b, act_=(yaT_hi, yaT_lo), nk=4)
                    pe.wait_ge(oblo_ready, NP_)
                    project(u, U_UP + m, b + 1, act_=(obT_hi, obT_lo), k0=4, nk=4).then_inc(w_used, 1)

            def by_rows(u, fourth, k, start, stop):
                q = fourth % NSPL
                take(u)
                pe.wait_ge(mixlo_ready, k + 1)
                for n, t in enumerate(WO_ORDER):
                    if k == 0 and t == 0:
                        pe.wait_ge(gmul_ready, KD + 2)
                    ts = slice(t * P, (t + 1) * P)
                    for h in range(2):
                        w = slice(512 * h, 512 * h + 512)
                        ins = three(PS[:, 2 * t + h, :], mixT_hi[:, k, ts], mixT_lo[:, k, ts], w_hi[:, q, w],
                                    w_lo[:, q, w], start, stop)
                    if stop and n < TT - 1:
                        ins.then_inc(wo_mm, 1)
                ins.then_inc(w_used, 1)

            for k in range(KD):
                by_rows(U_WO + k, U_WO + k, k, k == 0, k == KD - 1)
            pe.wait_ge(x2_ready, TT)
            transposes(1, xn2, WO_ORDER)

            with pe.Fori(0, FT // 2) as i:
                for j in range(2):
                    k = 2 * i + j
                    for g in range(2):
                        u = U_FI + 4 * i + 2 * j + g
                        f = U_FI + 2 * j + g
                        take(u)
                        if g == 0:
                            pe.wait_ge(prod_ready, k + 1)
                        project(u, f, 2 * j + g, fresh=KD if j == g == 0 else None).then_inc(w_used, 1)

            def down(u, fourth, k, start, stop):
                q = fourth % NSPL
                take(u)
                for m in Z_ORDER:
                    if start and m == 0:
                        pe.wait_ge(prod_ready, FT + 2)
                    w = slice(m * P, (m + 1) * P)
                    rows = (act_hi[:, k, :], act_lo[:, k, :]) if isinstance(k, int) else \
                        tuple(a[:, bass.ds(k, 1), :].rearrange("p a b -> p (a b)") for a in (act_hi, act_lo))
                    ins = three(PS[:, m, :], w_hi[:, q, w], w_lo[:, q, w], rows[0], rows[1], start, stop)
                    if stop:
                        ins.then_inc(z_mm_out, 1)
                if not stop:
                    ins.then_inc(w_used, 1)

            pe.wait_ge(actlo_ready, 1)
            down(U_FO, U_FO, 0, True, False)
            pe.wait_ge(actlo_ready, FT)
            with pe.Fori(0, (FT - 2) // 4) as i:
                for j in range(4):
                    down(U_FO + 1 + 4 * i + j, U_FO + 1 + j, 4 * i + 1 + j, False, False)
            down(U_FO + FT - 1, U_FO + FT - 1, FT - 1, False, True)
            pe.wait_ge(zT_ready, KD)
            for t in range(TT):
                for m in range(KD):
                    ins = pe.transpose(PS[:, 2 * t + m // 4, (m % 4) * P:(m % 4 + 1) * P],
                                       zT[:, m, t * P:(t + 1) * P], ident[:])
                ins.then_inc(z_T, 1)


_INS = ["x", "norm_mix_g", "w_in", "mu_shift", "w0", "w_decay_up", "a0", "w_iclr_up", "w_gate_up", "k_k", "k_a",
        "r_k", "ln_x_w", "ln_x_b", "w_up_a", "w_up_b", "w_o", "norm_ffn_g", "w_ffn_in", "w_ffn_out", "norm_final_g"]


def kernel(**inputs):
    import numpy as _np
    import concourse.bacc as _bacc
    from concourse import mybir as _mybir
    from concourse.bass_utils import run_bass_kernel_spmd as _run

    nc = _bacc.Bacc("TRN2", target_bir_lowering=False, num_devices=1)
    arrays, args = {}, []
    for name in _INS:
        a = _np.ascontiguousarray(inputs[name])
        arrays[f"in_{name}_dram"] = a
        args.append(nc.dram_tensor(f"in_{name}_dram", a.shape, _mybir.dt.from_np(a.dtype), kind="ExternalInput").ap())
    args.append(nc.dram_tensor("out_0_dram", (1, T, D), _mybir.dt.float32, kind="ExternalOutput").ap())
    build(nc, *args)
    r = _run(nc, [arrays], core_ids=[0])
    return r.results[0]["out_0_dram"]
```
